# Optimizing a Trainium2 kernel written in Bass

```python
import math
import jax
import jax.numpy as jnp
from jax import lax
import numpy as np

D_MODEL = 1024
BATCH = 1
SEQ = 512
DEPTH = 2

N_META = 16
HG_HEADS = 8
HG_KDIM = 128
HG_VDIM = 128
HG_WIDTH = HG_HEADS * HG_VDIM
HG_QK_WIDTH = HG_HEADS * HG_KDIM
CHUNK = 16
AT_HEADS = 8
AT_HEAD_DIM = 64
AT_WIDTH = AT_HEADS * 2 * AT_HEAD_DIM
MIX_WIDTH = HG_WIDTH + AT_WIDTH
Q_BLOCK = 128
ROPE_THETA = 10000.0
NORM_EPS = 1e-6
F_FLOOR = 1e-30
IN_COLS = (HG_QK_WIDTH, HG_QK_WIDTH, HG_QK_WIDTH, HG_WIDTH, HG_WIDTH,
           AT_WIDTH, AT_WIDTH, AT_WIDTH, AT_WIDTH)
IN_WIDTH = 9216

kernel_name = "hymba_hgrn2_diffattn_encoder"

def rmsnorm(x, g):
    xf = x.astype(jnp.float32)
    ms = jnp.mean(xf * xf, axis=-1, keepdims=True)
    return xf * lax.rsqrt(ms + NORM_EPS) * g.astype(jnp.float32)

def rope_tables(L):
    inv = ROPE_THETA ** (-jnp.arange(0, AT_HEAD_DIM, 2, dtype=jnp.float32) / AT_HEAD_DIM)
    ang = jnp.arange(L, dtype=jnp.float32)[:, None] * inv[None, :]
    return jnp.cos(ang), jnp.sin(ang)

def apply_rope(t, cos, sin):
    tf = t.astype(jnp.float32)
    half = AT_HEAD_DIM // 2
    t1, t2 = tf[..., :half], tf[..., half:]
    c = cos[None, :, None, None, :]
    s = sin[None, :, None, None, :]
    return jnp.concatenate([t1 * c - t2 * s, t2 * c + t1 * s], axis=-1)

def hgrn2_chunk_scan(q, k, v, log_f):
    Bs, L, H, K = q.shape
    V = v.shape[-1]
    N = L // CHUNK
    q, k, log_f = (t.reshape(Bs, N, CHUNK, H, K) for t in (q, k, log_f))
    v = v.reshape(Bs, N, CHUNK, H, V)
    b = jnp.cumsum(log_f, axis=2)
    b_last = b[:, :, -1:]
    mask = jnp.tril(jnp.ones((CHUNK, CHUNK), dtype=bool))[:, :, None, None]
    diff = b[:, :, :, None] - b[:, :, None, :]
    dec = jnp.where(mask, jnp.exp(jnp.where(mask, diff, 0.0)), 0.0)
    att = jnp.einsum('bnthk,bnshk,bntshk->bnhts', q, k, dec)
    o_intra = jnp.einsum('bnhts,bnshv->bnthv', att, v)
    q_dec = q * jnp.exp(b)
    k_dec = k * jnp.exp(b_last - b)
    decay = jnp.exp(b_last[:, :, 0])

    def step(S, xs):
        qd, kd, vn, dn = xs
        o = jnp.einsum('bthk,bhkv->bthv', qd, S)
        S = dn[..., None] * S + jnp.einsum('bthk,bthv->bhkv', kd, vn)
        return S, o

    xs = (jnp.moveaxis(q_dec, 1, 0), jnp.moveaxis(k_dec, 1, 0),
          jnp.moveaxis(v, 1, 0), jnp.moveaxis(decay, 1, 0))
    S0 = jnp.zeros((Bs, H, K, V), jnp.float32)
    _, o_inter = lax.scan(step, S0, xs)
    o = o_intra + jnp.moveaxis(o_inter, 0, 1)
    return o.reshape(Bs, L, H, V)

def hgrn2_mixer(q, fz_fwd, fz_bwd, i_v, gate, lb, norm_gain):
    Bs, L = q.shape[:2]
    qh = q.reshape(Bs, L, HG_HEADS, HG_KDIM).astype(jnp.float32)
    vh = i_v.reshape(Bs, L, HG_HEADS, HG_VDIM).astype(jnp.float32)

    def gates(z, lb_dir):
        z = z.reshape(Bs, L, HG_HEADS, HG_KDIM).astype(jnp.float32)
        lb_dir = lb_dir.reshape(HG_HEADS, HG_KDIM)
        f = lb_dir + (1.0 - lb_dir) * jax.nn.sigmoid(z)
        k_in = (1.0 - lb_dir) * jax.nn.sigmoid(-z)
        log_f = jnp.log(jnp.maximum(f, F_FLOOR))
        return k_in, log_f

    k_f, a_f = gates(fz_fwd, lb[0])
    k_b, a_b = gates(fz_bwd, lb[1])
    flip = lambda t: jnp.flip(t, axis=1)
    o = hgrn2_chunk_scan(qh, k_f, vh, a_f) + \
        flip(hgrn2_chunk_scan(flip(qh), flip(k_b), flip(vh), flip(a_b)))
    g = gate.reshape(Bs, L, HG_HEADS, HG_VDIM).astype(jnp.float32)
    o = rmsnorm(o, norm_gain) * jax.nn.silu(g)
    return o.reshape(Bs, L, HG_WIDTH)

def diff_attention_mixer(q, k, v, gate, lam_vecs, subln_g, layer_idx, cos, sin):
    Bs, L = q.shape[:2]
    qh = apply_rope(q.reshape(Bs, L, AT_HEADS, 2, AT_HEAD_DIM), cos, sin)
    kh = apply_rope(k.reshape(Bs, L, AT_HEADS, 2, AT_HEAD_DIM), cos, sin)
    vh = v.reshape(Bs, L, AT_HEADS, 2 * AT_HEAD_DIM).astype(jnp.float32)
    lam_init = 0.8 - 0.6 * math.exp(-0.3 * layer_idx)
    lv = lam_vecs.astype(jnp.float32)
    lam = jnp.exp(jnp.sum(lv[0] * lv[1])) - jnp.exp(jnp.sum(lv[2] * lv[3])) + lam_init
    nb = -(-L // Q_BLOCK)
    pad = nb * Q_BLOCK - L
    qp = jnp.pad(qh, ((0, 0), (0, pad), (0, 0), (0, 0), (0, 0)))
    qb = qp.reshape(Bs, nb, Q_BLOCK, AT_HEADS, 2, AT_HEAD_DIM).transpose(1, 0, 2, 3, 4, 5)
    scale = AT_HEAD_DIM ** -0.5

    def block(qblk):
        s = jnp.einsum('bqhcd,bkhcd->bhcqk', qblk, kh) * scale
        p = jax.nn.softmax(s, axis=-1)
        p_diff = p[:, :, 0] - lam * p[:, :, 1]
        return jnp.einsum('bhqk,bkhv->bqhv', p_diff, vh)

    o = lax.map(block, qb)
    o = o.transpose(1, 0, 2, 3, 4).reshape(Bs, nb * Q_BLOCK, AT_HEADS, 2 * AT_HEAD_DIM)[:, :L]
    g = gate.reshape(Bs, L, AT_HEADS, 2 * AT_HEAD_DIM).astype(jnp.float32)
    o = rmsnorm(o, subln_g) * (1.0 - lam_init) * jax.nn.silu(g)
    return o.reshape(Bs, L, AT_WIDTH)

def setup_inputs(seed: int = 0) -> dict:
    key = jax.random.key(seed)
    ks = jax.random.split(key, 10)
    f32 = jnp.float32
    return {
        "x": jax.random.normal(ks[0], (BATCH, SEQ, D_MODEL), f32),
        "meta_tokens": jax.random.normal(ks[1], (N_META, D_MODEL), f32),
        "norm_g": 1.0 + 0.02 * jax.random.normal(ks[2], (DEPTH, D_MODEL), f32),
        "w_in": jax.random.normal(ks[3], (DEPTH, D_MODEL, IN_WIDTH), f32) * D_MODEL ** -0.5,
        "hg_lb_logits": jax.random.normal(ks[4], (DEPTH, 2, HG_QK_WIDTH), f32),
        "hg_norm_g": 1.0 + 0.02 * jax.random.normal(ks[5], (DEPTH, HG_VDIM), f32),
        "diff_lambda": 0.1 * jax.random.normal(ks[6], (DEPTH, 4, AT_HEAD_DIM), f32),
        "diff_subln_g": 1.0 + 0.02 * jax.random.normal(ks[7], (DEPTH, 2 * AT_HEAD_DIM), f32),
        "w_out": jax.random.normal(ks[8], (DEPTH, MIX_WIDTH, D_MODEL), f32) * MIX_WIDTH ** -0.5,
        "final_norm_g": 1.0 + 0.02 * jax.random.normal(ks[9], (D_MODEL,), f32),
    }

def reference(x, meta_tokens, norm_g, w_in, hg_lb_logits, hg_norm_g, diff_lambda,
              diff_subln_g, w_out, final_norm_g):
    dtype = x.dtype
    Bs = x.shape[0]
    meta = jnp.broadcast_to(meta_tokens[None].astype(dtype), (Bs, N_META, D_MODEL))
    h = jnp.concatenate([meta, x], axis=1)
    L = h.shape[1]
    cos, sin = rope_tables(L)
    lbp = jax.nn.softmax(hg_lb_logits.astype(jnp.float32), axis=0)
    lbs = jnp.cumsum(lbp, axis=0) - lbp[0:1]
    split_idx = [int(s) for s in np.cumsum(IN_COLS)[:-1]]
    for l in range(DEPTH):
        u = rmsnorm(h, norm_g[l]).astype(dtype)
        p = u @ w_in[l]
        hq, hf_f, hf_b, hi, hgt, aq, ak, av, agt = jnp.split(p, split_idx, axis=-1)
        o_h = hgrn2_mixer(hq, hf_f, hf_b, hi, hgt, lbs[l], hg_norm_g[l])
        o_a = diff_attention_mixer(aq, ak, av, agt, diff_lambda[l], diff_subln_g[l], l, cos, sin)
        mixed = jnp.concatenate([o_h, o_a], axis=-1).astype(dtype)
        h = h + mixed @ w_out[l]
    out = rmsnorm(h, final_norm_g).astype(dtype)
    return out[:, N_META:]


_drawn_inputs = setup_inputs


def setup_inputs(seed=0):
    import zlib

    import numpy as np

    out = dict(_drawn_inputs(seed))
    spreads = {}
    factors = {'hg_norm_g': 4.737, 'diff_subln_g': 6.23, 'final_norm_g': 2.855}
    for name, (base, spread) in spreads.items():
        noise = np.random.default_rng([zlib.crc32(name.encode()), seed]).standard_normal(out[name].shape)
        drawn = base * np.exp(spread * noise) if base else spread * noise
        out[name] = jnp.asarray(drawn.astype(out[name].dtype))
    for name, factor in factors.items():
        out[name] = (out[name] * factor).astype(out[name].dtype)
    return out
```

```python
import math
from contextlib import ExitStack

import concourse.bass as bass
import numpy as np
from concourse import mybir

P = 128
DEPTH = 2
D_MODEL = 1024
N_META = 16
SEQ = 512
T = N_META + SEQ
HALF = T // 2
HG_HEADS = 8
AT_HEADS = 8
AT_HEAD_DIM = 64
HEADS = HG_HEADS + AT_HEADS
KT = D_MODEL // P
IN_TILES = 9216 // P
OUT_TILES = D_MODEL // P
NORM_EPS = 1e-6
F_FLOOR = 1e-30
ROPE_THETA = 10000.0
N_CHUNKS = SEQ // P
LEVELS = 8
META_LEVELS = 5
HG_TILES = ("zf", "zb", "q", "v", "g")
AT_TILES = ("aq", "ak", "av", "ag")
STAGE_USE = {"zf": 0, "zb": 1, "g": 2, "aq": 0, "ak": 1, "ag": 2}

TOTALS_AT = {}
_at = 0
for _m in (2, 4, 8, 16, 32, 64, 128):
    TOTALS_AT[_m] = _at
    _at += T // _m
TOTALS = _at


def layer_units():
    units = []
    for c in range(HEADS):
        if c == HG_HEADS + 1:
            units += [("outA", c, j) for j in range(OUT_TILES)]
        units += [(what, c, i) for i, what in enumerate(HG_TILES if c < HG_HEADS else AT_TILES)]
    return units + [("outB", HEADS, j) for j in range(OUT_TILES)]


UNITS = layer_units()
LAYER_UNITS = len(UNITS)
FIRST_UNIT = {c: next(i for i, u in enumerate(UNITS) if u[1] == c and u[0] not in ("outA", "outB"))
              for c in range(HEADS)}
OUT_B = LAYER_UNITS - OUT_TILES

HG_STEPS = 1 + LEVELS + 4
AT_STEPS = 2 * 7 + 1


def steps_of(c):
    return HG_STEPS if c < HG_HEADS else AT_STEPS


def fed_units(c):
    if c == HEADS - 1:
        return OUT_B, OUT_B
    first = FIRST_UNIT[c] + (len(HG_TILES) if c < HG_HEADS else len(AT_TILES))
    last = FIRST_UNIT[c + 1] + (len(HG_TILES) if c + 1 < HG_HEADS else len(AT_TILES))
    return first, last


def pieces_by(c, s):
    if s < 0:
        return 0
    first, last = fed_units(c)
    return (s + 1) * (last - first) * KT // steps_of(c)


def units_after(c, s):
    first, _ = fed_units(c)
    return range(first + pieces_by(c, s - 2) // KT, first + pieces_by(c, s - 1) // KT)


def encoder_trunk(nc, x_t, w_units, norm_g, lb_logits, hg_gain, lambdas, at_gain, final_g,
                  level_masks, identity, rope, out_t):
    f32 = mybir.dt.float32
    f32r = mybir.dt.float32r
    i32 = mybir.dt.int32
    ALU = mybir.AluOpType
    ACT = mybir.ActivationFunctionType
    X = mybir.AxisListType.X

    N_RAW = 2
    N_CUT = 3

    ctx = ExitStack()
    with ctx:
        def sb(name, shape, dt=f32):
            return ctx.enter_context(nc.sbuf_tensor(name, shape, dt))

        def sem(name):
            return ctx.enter_context(nc.semaphore(name))

        h = sb("h", [P, KT, T])
        u_hi = sb("u_hi", [P, KT, T], f32r)
        u_lo = sb("u_lo", [P, KT, T], f32r)
        mix_hi = sb("mix_hi", [P, 8, T], f32r)
        mix_lo = sb("mix_lo", [P, 8, T], f32r)
        w_raw = sb("w_raw", [P, N_RAW, KT, P])
        w_hi = sb("w_hi", [P, N_CUT, KT, P], f32r)
        w_lo = sb("w_lo", [P, N_CUT, KT, P], f32r)
        masks = sb("masks", [P, LEVELS, P], i32)
        ident = sb("ident", [P, P])
        ones = sb("ones", [P, P])
        cos_sin = sb("cos_sin", [P, 2, T])
        g_in = sb("g_in", [P, DEPTH, KT])
        g_final = sb("g_final", [P, KT])
        g_hg = sb("g_hg", [P, DEPTH])
        g_at = sb("g_at", [P, DEPTH])
        lb = sb("lb", [P, DEPTH, 2 * HG_HEADS])
        one_minus_lb = sb("one_minus_lb", [P, DEPTH, 2 * HG_HEADS])
        lb_work = sb("lb_work", [P, 4, 2 * HG_HEADS])
        lam_in = sb("lam_in", [P, DEPTH * 2, 2, AT_HEAD_DIM])
        lam_prod = sb("lam_prod", [P, DEPTH * 2, AT_HEAD_DIM])
        lam_sum = sb("lam_sum", [P, DEPTH, 2])
        lam = sb("lam", [P, DEPTH])
        stage = sb("stage", [P, 2, 2, T])
        gate_f = sb("gate_f", [P, 3, T])
        totals = sb("totals", [P, 3, TOTALS])
        decay = sb("decay", [P, 4, T])
        qkk = sb("qkk", [P, 2, 3, T])
        qk_dec = sb("qk_dec", [P, 2, 2, T])
        gates = sb("gates", [P, 2, T])
        v_t = sb("v_t", [P, T])
        v_main = sb("v_main", [P, N_CHUNKS, P])
        v_meta = sb("v_meta", [N_META, P])
        cols = sb("cols", [P, 2 * N_CHUNKS + 2, P])
        state_f = sb("state_f", [P, N_CHUNKS, P])
        state_b = sb("state_b", [P, N_CHUNKS, P])
        score = sb("score", [P, N_CHUNKS, P])
        score_meta = sb("score_meta", [N_META, N_META])
        o_t = sb("o_t", [P, T])
        sq = sb("sq", [P, T])
        eps_count = sb("eps_count", [P, 2])
        neg_max = sb("neg_max", [P, 2, 2])
        row_sum = sb("row_sum", [P, 2, 2])
        row_inv = sb("row_inv", [P, 2, 2])

        proj = [ctx.enter_context(nc.psum_tensor(f"proj{i}", [P, 2, 512], f32)) for i in range(2)]
        pair = ctx.enter_context(nc.psum_tensor("pair", [P, 2, 512], f32))
        main = ctx.enter_context(nc.psum_tensor("main", [P, 512], f32))
        meta = ctx.enter_context(nc.psum_tensor("meta", [P, 512], f32))

        consts_in = sem("consts_in")
        x_in = sem("x_in")
        raw_in = [sem(f"raw_in{i}") for i in range(N_RAW)]
        out_stored = sem("out_stored")
        ones_set = sem("ones_set")
        hi_cut = sem("hi_cut")
        lo_cut = sem("lo_cut")
        unit_done = sem("unit_done")
        evacuated = [sem(f"evacuated{i}") for i in range(2)]
        stage_read = sem("stage_read")
        decay_set = sem("decay_set")
        qk_ready = sem("qk_ready")
        level_done = sem("level_done")
        level_read = sem("level_read")
        meta_read = sem("meta_read")
        v_turned = sem("v_turned")
        v_ready = sem("v_ready")
        k_turned = sem("k_turned")
        k_ready = sem("k_ready")
        kv_done = sem("kv_done")
        states_ready = sem("states_ready")
        o_done = sem("o_done")
        sq_ready = sem("sq_ready")
        sq_summed = sem("sq_summed")
        root_ready = sem("root_ready")
        mixed = sem("mixed")
        mix_hi_ready = sem("mix_hi_ready")
        mix_lo_ready = sem("mix_lo_ready")
        s_done = sem("s_done")
        max_ready = sem("max_ready")
        exp_done = sem("exp_done")
        p_ready = sem("p_ready")
        p_turned = sem("p_turned")
        pt_ready = sem("pt_ready")
        pv_done = sem("pv_done")
        pv_read = sem("pv_read")
        h_sq = sem("h_sq")
        h_sq_summed = sem("h_sq_summed")
        u_ready = sem("u_ready")
        u_hi_ready = sem("u_hi_ready")
        u_lo_ready = sem("u_lo_ready")
        out_ready = sem("out_ready")
        lb_exp = sem("lb_exp")
        lb_max = sem("lb_max")
        act_step = sem("act_step")
        dve_step = sem("dve_step")

        halves = (slice(0, HALF), slice(HALF, T))
        both = slice(0, HALF)

        def chunk(c):
            return slice(N_META + c * P, N_META + (c + 1) * P)

        def evac_count(t):
            return t // 2 + 1

        def two(ap):
            return ap.rearrange("p (h n) -> p h n", h=2)

        def block_half(x, m, half):
            first = 0 if m < N_META else N_META
            return x[:, :, first:T].rearrange("p a (b h m) -> p a b h m", h=2, m=m)[:, :, :, half, :]

        def block_totals(a, m, half):
            n = (T if m <= N_META else SEQ) // m
            skip = 1 if m == N_META else 0
            src = gate_f[:, a, 0:T] if m == 1 else \
                totals[:, a, TOTALS_AT[m] + skip:TOTALS_AT[m] + n]
            return src.rearrange("p a (b h) -> p a b h", h=2)[:, :, :, half]

        def u_out(k):
            if k < 4:
                return decay[:, k, N_META:T]
            return qkk[:, (k - 4) // 2, (k - 4) % 2, N_META:T]

        block = ctx.enter_context(nc.Block())

        @block.sync
        def _(sp):
            for k in range(KT):
                sp.dma_start(h[:, k, :], x_t[:, k, :]).then_inc(x_in, 16)
            sp.dma_start(g_in[:, :, :], norm_g).then_inc(x_in, 16)
            for u in range(DEPTH * LAYER_UNITS):
                if u == N_RAW:
                    for dst, src in ((ident[:, :], identity), (lb[:, :, :], lb_logits), (g_hg[:, :], hg_gain),
                                     (g_at[:, :], at_gain), (g_final[:, :], final_g),
                                     (masks[:, :, :], level_masks), (cos_sin[:, :, :], rope),
                                     (lam_in[:, :, :, :], lambdas)):
                        sp.dma_start(dst, src).then_inc(consts_in, 16)
                if u >= N_RAW:
                    sp.wait_ge(lo_cut, u - N_RAW + 1)
                sp.dma_start(w_raw[:, u % N_RAW, :, :], w_units[u]).then_inc(raw_in[u % N_RAW], 16)
            for k in range(KT):
                sp.wait_ge(out_ready, k + 1)
                sp.dma_start(out_t[k], u_out(k)).then_inc(out_stored, 16)
            sp.wait_ge(out_stored, 16 * KT)

        @block.gpsimd
        def _(pool):
            pool.memset(ones[:, :], 1.0).then_inc(ones_set, 1)
            pool.memset(eps_count[:, 0:1], D_MODEL * NORM_EPS).then_inc(ones_set, 1)
            pool.memset(eps_count[:, 1:2], P * NORM_EPS).then_inc(ones_set, 1)

            def cut_low(u):
                pool.wait_ge(hi_cut, u + 1)
                pool.tensor_tensor(w_lo[:, u % N_CUT, :, :], w_raw[:, u % N_RAW, :, :],
                                   w_hi[:, u % N_CUT, :, :].bitcast(f32), ALU.subtract)\
                    .then_inc(lo_cut, 1)

            def set_decay(l, c):
                g = l * HG_HEADS + c
                pool.wait_ge(stage_read, 3 * (l * HEADS + c) + 2)
                if g > 0:
                    pool.wait_ge(qk_ready, 10 * g)
                pool.memset(decay[:, 1, :], 1.0).then_inc(decay_set, 1)
                pool.memset(decay[:, 3, :], 1.0).then_inc(decay_set, 1)
                pool.tensor_copy(decay[:, 0, :], gate_f[:, 0, :]).then_inc(decay_set, 1)
                pool.tensor_copy(decay[:, 2, :], gate_f[:, 1, :]).then_inc(decay_set, 1)

            def cut_mixed(l, c):
                pool.wait_ge(mix_hi_ready, l * HEADS + c + 1)
                pool.tensor_tensor(mix_lo[:, c % 8, :], o_t[:, :],
                                   mix_hi[:, c % 8, :].bitcast(f32), ALU.subtract)\
                    .then_inc(mix_lo_ready, 1)

            for u in range(N_CUT):
                cut_low(u)
            for l in range(DEPTH):
                base = l * LAYER_UNITS

                def follow(units):
                    for i in units:
                        if base + i + N_CUT < DEPTH * LAYER_UNITS:
                            cut_low(base + i + N_CUT)

                follow(range(len(HG_TILES)))
                set_decay(l, 0)
                for c in range(HEADS):
                    for s in range(steps_of(c)):
                        follow(units_after(c, s))
                    follow(units_after(c, steps_of(c)))
                    if c + 1 < HG_HEADS:
                        set_decay(l, c + 1)
                    cut_mixed(l, c)
                follow(range(OUT_B, LAYER_UNITS))

        @block.scalar
        def _(act):
            own = [0]

            def step(ins):
                own[0] += 1
                ins.then_inc(act_step, 1)
                return own[0]

            def cut_high(u):
                act.wait_ge(raw_in[u % N_RAW], 16 * (u // N_RAW + 1))
                if u >= N_CUT:
                    act.wait_ge(unit_done, u - N_CUT + 1)
                act.activation(w_hi[:, u % N_CUT, :, :], w_raw[:, u % N_RAW, :, :], ACT.Copy)\
                    .then_inc(hi_cut, 1)

            def square_h(n, k):
                if n == 0:
                    act.wait_ge(x_in, 16 * (KT + 1))
                else:
                    t = (n - 1) * LAYER_UNITS + OUT_B + k
                    act.wait_ge(evacuated[t % 2], evac_count(t))
                if k >= 4:
                    act.wait_ge(h_sq_summed, n * KT + k - 4 + 1)
                act.activation(decay[:, k % 4, :], h[:, k, :], ACT.Square).then_inc(h_sq, 1)

            def root(eps):
                act.activation(two(sq[:, :]), pair[:, :, both], ACT.Sqrt, bias=eps_count[:, eps:eps + 1])\
                    .then_inc(root_ready, 1)

            def cut_u(l):
                act.wait_ge(h_sq_summed, (l + 1) * KT)
                root(0)
                if l == DEPTH:
                    return
                for k in range(KT):
                    act.wait_ge(u_ready, l * KT + k + 1)
                    act.activation(u_hi[:, k, :], qk_dec[:, (k % 4) // 2, k % 2, :], ACT.Copy)\
                        .then_inc(u_hi_ready, 1)

            def evacuate(l, i):
                what, c, j = UNITS[i]
                t = l * LAYER_UNITS + i
                src = proj[t % 2][:, :, both]
                if what in ("outA", "outB"):
                    act.wait_ge(unit_done, t + 1)
                else:
                    act.wait_ge(unit_done, t + 1)
                    use = (l * HEADS + c) * 3 + STAGE_USE.get(what, 0)
                    if what not in ("q", "v", "av") and use >= 2:
                        act.wait_ge(stage_read, use - 1)
                    a, b = two(stage[:, use % 2, 0, :]), two(stage[:, use % 2, 1, :])
                    done = evacuated[t % 2]
                    if what in ("zf", "zb"):
                        step(act.activation(a, src, ACT.Sigmoid))
                        act.activation(b, src, ACT.Sigmoid, scale=-1.0).then_inc(done, 1)
                    elif what == "q":
                        act.activation(two(qkk[:, c % 2, 0, :]), src, ACT.Copy).then_inc(done, 1)
                    elif what in ("v", "av"):
                        act.activation(two(v_t[:, :]), src, ACT.Copy).then_inc(done, 1)
                    elif what in ("g", "ag"):
                        if what == "g":
                            step(act.activation(a, src, ACT.Sigmoid))
                        else:
                            step(act.activation(a, src, ACT.Tanh, scale=0.5))
                        act.activation(b, src, ACT.Copy).then_inc(done, 1)
                    else:
                        act.activation(a, src, ACT.Copy,
                                       scale=AT_HEAD_DIM ** -0.5 if what == "aq" else 1.0)\
                            .then_inc(done, 1)
                if t + N_CUT < DEPTH * LAYER_UNITS:
                    cut_high(t + N_CUT)

            def copy_v(n):
                act.wait_ge(v_turned, n + 1)
                step(act.activation(v_main[:, :, :], main[:, :].rearrange("p (c n) -> p c n", c=4), ACT.Copy))
                act.activation(v_meta[:, :], meta[0:N_META, 0:P], ACT.Copy).then_inc(v_ready, 1)

            def hgrn(l, c, s):
                n, g = l * HEADS + c, l * HG_HEADS + c
                if s == 0:
                    copy_v(n)
                if s == LEVELS + 1:
                    act.wait_ge(k_turned, 2 * g + 1)
                    act.activation(cols[:, 0:4, :], pair[:, 0, :].rearrange("p (c n) -> p c n", c=4),
                                   ACT.Copy).then_inc(k_ready, 1)
                    act.wait_ge(k_turned, 2 * g + 2)
                    step(act.activation(cols[:, 4:7, :],
                                        pair[:, 1, 0:3 * P].rearrange("p (c n) -> p c n", c=3), ACT.Copy))
                    act.activation(cols[0:N_META, 7, :], meta[0:N_META, 0:P], ACT.Copy)\
                        .then_inc(k_ready, 1)
                if s == LEVELS + 3:
                    if n > 0:
                        act.wait_ge(mix_lo_ready, n)
                    act.wait_ge(o_done, g + 1)
                    step(act.activation(o_t[:, N_META:T], main[:, :], ACT.Copy))
                    w = step(act.activation(o_t[:, 0:N_META], meta[:, 0:N_META], ACT.Copy))
                    act.wait_ge(act_step, w)
                    act.activation(sq[:, :], o_t[:, :], ACT.Square).then_inc(sq_ready, 1)

            def attend(l, c, s):
                n, a = l * HEADS + c, l * AT_HEADS + c - HG_HEADS
                i, comp = s // 2, s % 2
                if s == 0:
                    copy_v(n)
                if i < 5:
                    rows = P if i < 4 else N_META
                    if comp == 0 and i >= 2:
                        act.wait_ge(p_ready, a * 5 + i - 1)
                    act.wait_ge(max_ready, a * 10 + 2 * i + comp + 1)
                    act.activation(two(decay[0:rows, 2 * (i % 2) + comp, :]), pair[0:rows, :, both],
                                   ACT.Exp, bias=neg_max[0:rows, i % 2, comp:comp + 1],
                                   accum_out=row_sum[0:rows, i % 2, comp:comp + 1]).then_inc(exp_done, 1)
                if comp == 0 and 2 <= i < 7:
                    j = i - 2
                    cs = chunk(j) if j < 4 else slice(0, N_META)
                    rows = P if j < 4 else N_META
                    if j == 0:
                        act.wait_ge(mix_lo_ready, n)
                    act.wait_ge(pv_done, a * 5 + j + 1)
                    act.activation(o_t[:, cs], meta[:, 0:rows], ACT.Copy).then_inc(pv_read, 1)
                if comp == 1 and 1 <= i < 6:
                    j = i - 1
                    rows = P if j < 4 else N_META
                    act.wait_ge(p_turned, a * 5 + j + 1)
                    step(act.activation(cols[:, 0:4, 0:rows],
                                        main[:, :].rearrange("p (c n) -> p c n", c=4)[:, :, 0:rows],
                                        ACT.Copy))
                    act.activation(cols[0:N_META, 4, 0:rows], meta[0:N_META, 0:rows], ACT.Copy)\
                        .then_inc(pt_ready, 1)
                if s == 13:
                    act.wait_ge(pv_read, 5 * (a + 1))
                    act.activation(sq[:, :], o_t[:, :], ACT.Square).then_inc(sq_ready, 1)

            def round_mixed(l, c):
                n = l * HEADS + c
                act.wait_ge(sq_summed, n + 1)
                root(1)
                if c >= HG_HEADS:
                    act.wait_ge(unit_done, l * LAYER_UNITS + FIRST_UNIT[HG_HEADS + 1])
                act.wait_ge(mixed, n + 1)
                act.activation(mix_hi[:, c % 8, :], o_t[:, :], ACT.Copy).then_inc(mix_hi_ready, 1)

            act.wait_ge(ones_set, 3)
            for u in range(N_RAW):
                cut_high(u)
            for k in range(KT):
                square_h(0, k)
            for u in range(N_RAW, N_CUT):
                cut_high(u)
            for l in range(DEPTH):
                cut_u(l)
                if l == 0:
                    act.wait_ge(lb_max, 1)
                    act.activation(lb_work[:, 0:2, :], lb_work[:, 0:2, :], ACT.Exp).then_inc(lb_exp, 1)
                    act.wait_ge(lb_max, 2)
                    act.activation(lam_sum[:, :, :], lam_sum[:, :, :], ACT.Exp).then_inc(lb_exp, 1)
                for i in range(len(HG_TILES)):
                    evacuate(l, i)
                for c in range(HEADS):
                    for s in range(steps_of(c)):
                        (hgrn if c < HG_HEADS else attend)(l, c, s)
                        for i in units_after(c, s):
                            evacuate(l, i)
                    for i in units_after(c, steps_of(c)):
                        evacuate(l, i)
                    round_mixed(l, c)
                for i in range(OUT_B, LAYER_UNITS):
                    evacuate(l, i)
                    square_h(l + 1, i - OUT_B)
            cut_u(DEPTH)

        @block.vector
        def _(dve):
            own = [0]

            def step(ins):
                own[0] += 1
                ins.then_inc(dve_step, 1)
                return own[0]

            def after(w):
                dve.wait_ge(dve_step, w)

            def prepare_lower_bounds():
                dve.wait_ge(consts_in, 16 * 8)
                w = step(dve.tensor_tensor(lb_work[:, 2, :], lb[:, 0, :], lb[:, 1, :], ALU.max))
                after(w)
                step(dve.tensor_tensor(lb_work[:, 0, :], lb[:, 0, :], lb_work[:, 2, :], ALU.subtract))
                dve.tensor_tensor(lb_work[:, 1, :], lb[:, 1, :], lb_work[:, 2, :], ALU.subtract)\
                    .then_inc(lb_max, 1)
                w = step(dve.tensor_tensor(lam_prod[:, :, :], lam_in[:, :, 0, :], lam_in[:, :, 1, :],
                                           ALU.mult))
                after(w)
                dve.tensor_reduce(lam_sum[:, :, :].rearrange("p a b -> p (a b)"), lam_prod[:, :, :],
                                  axis=X, op=ALU.add).then_inc(lb_max, 1)
                dve.wait_ge(lb_exp, 1)
                w = step(dve.tensor_tensor(lb_work[:, 2, :], lb_work[:, 0, :], lb_work[:, 1, :], ALU.add))
                after(w)
                w = step(dve.reciprocal(lb_work[:, 3, :], lb_work[:, 2, :]))
                after(w)
                step(dve.tensor_tensor(lb_work[:, 0, :], lb_work[:, 0, :], lb_work[:, 3, :], ALU.mult))
                w = step(dve.tensor_tensor(lb_work[:, 1, :], lb_work[:, 1, :], lb_work[:, 3, :], ALU.mult))
                after(w)
                w = step(dve.tensor_tensor(lb_work[:, 2, :], lb_work[:, 0, :], lb_work[:, 1, :], ALU.add))
                after(w)
                step(dve.tensor_tensor(lb[:, 0, :], lb_work[:, 0, :], lb_work[:, 0, :], ALU.subtract))
                w = step(dve.tensor_tensor(lb[:, 1, :], lb_work[:, 2, :], lb_work[:, 0, :], ALU.subtract))
                after(w)
                step(dve.tensor_scalar(one_minus_lb[:, :, :], lb[:, :, :], -1.0, 1.0, ALU.mult, ALU.add))
                dve.wait_ge(lb_exp, 2)
                for l in range(DEPTH):
                    init = 0.8 - 0.6 * math.exp(-0.3 * l)
                    w = step(dve.tensor_tensor(lam[:, l:l + 1], lam_sum[:, l, 0:1], lam_sum[:, l, 1:2],
                                               ALU.subtract))
                    after(w)
                    step(dve.tensor_scalar(lam[:, l:l + 1], lam[:, l:l + 1], init, None, ALU.add))
                    step(dve.tensor_scalar(g_at[:, l:l + 1], g_at[:, l:l + 1],
                                           math.sqrt(P) * (1.0 - init) * 0.5, None, ALU.mult))
                step(dve.tensor_scalar(g_hg[:, :], g_hg[:, :], math.sqrt(P), None, ALU.mult))
                w = step(dve.tensor_scalar(g_final[:, :], g_final[:, :], math.sqrt(D_MODEL), None, ALU.mult))
                after(w)

            def inverse_rms(roots):
                dve.wait_ge(root_ready, roots)
                return step(dve.reciprocal(sq[:, :], sq[:, :]))

            def norm_u(l):
                after(inverse_rms(l * (HEADS + 1) + 1))
                for k in range(KT + 1):
                    if k < KT:
                        if k >= 4:
                            dve.wait_ge(u_lo_ready, l * KT + k - 4 + 1)
                        dve.scalar_tensor_tensor(qk_dec[:, (k % 4) // 2, k % 2, :], h[:, k, :],
                                                 g_in[:, l, k:k + 1], sq[:, :], ALU.mult, ALU.mult)\
                            .then_inc(u_ready, 1)
                    if k > 0:
                        j = k - 1
                        dve.wait_ge(u_hi_ready, l * KT + j + 1)
                        dve.tensor_tensor(u_lo[:, j, :], qk_dec[:, (j % 4) // 2, j % 2, :],
                                          u_hi[:, j, :].bitcast(f32), ALU.subtract)\
                            .then_inc(u_lo_ready, 1)

            def norm_out():
                after(inverse_rms(DEPTH * (HEADS + 1) + 1))
                for k in range(KT):
                    dve.scalar_tensor_tensor(u_out(k), h[:, k, N_META:T], g_final[:, k:k + 1],
                                             sq[:, N_META:T], ALU.mult, ALU.mult).then_inc(out_ready, 1)

            def follow(l, i):
                what, c, j = UNITS[i]
                t = l * LAYER_UNITS + i
                n = l * HEADS + c
                if what in ("outA", "outB"):
                    dve.wait_ge(unit_done, t + 1)
                    dve.tensor_tensor(two(h[:, j, :]), two(h[:, j, :]), proj[t % 2][:, :, both], ALU.add)\
                        .then_inc(evacuated[t % 2], 1)
                    return
                if what in ("q", "v", "av"):
                    return
                use = n * 3 + STAGE_USE[what]
                dve.wait_ge(evacuated[t % 2], evac_count(t))
                if use:
                    dve.wait_ge(stage_read, use)
                a, b = stage[:, use % 2, 0, :], stage[:, use % 2, 1, :]
                if what in ("zf", "zb"):
                    d = 0 if what == "zf" else 1
                    row = d * HG_HEADS + c
                    oml = one_minus_lb[:, l, row:row + 1]
                    w = step(dve.tensor_scalar(a, a, oml, lb[:, l, row:row + 1], ALU.mult, ALU.add))
                    step(dve.tensor_scalar(qkk[:, c % 2, 1 + d, :], b, oml, None, ALU.mult))
                    after(w)
                    if d == 0:
                        step(dve.tensor_scalar(gate_f[:, 2, :], a, F_FLOOR, None, ALU.max))
                    dve.tensor_scalar(gate_f[:, d, :], a, F_FLOOR, None, ALU.max)\
                        .then_inc(stage_read, 1)
                elif what == "g":
                    dve.tensor_tensor(gates[:, c % 2, :], a, b, ALU.mult).then_inc(stage_read, 1)
                elif what == "ag":
                    dve.scalar_tensor_tensor(gates[:, c % 2, :], a, 1.0, b, ALU.add, ALU.mult)\
                        .then_inc(stage_read, 1)
                else:
                    d = 0 if what == "aq" else 1
                    w1 = step(dve.stream_shuffle(b, a, [r ^ 1 for r in range(32)]))
                    step(dve.tensor_tensor(gate_f[:, 0, :], a, cos_sin[:, 0, :], ALU.mult))
                    after(w1)
                    w = step(dve.tensor_tensor(gate_f[:, 1, :], b, cos_sin[:, 1, :], ALU.mult))
                    after(w)
                    dve.tensor_tensor(qkk[:, c % 2, d, :], gate_f[:, 0, :], gate_f[:, 1, :], ALU.add)\
                        .then_inc(stage_read, 1)

            def copy_level(g, lv):
                dve.wait_ge(level_done, g * LEVELS + lv + 1)
                src = pair[:, lv % 2, :].rearrange("p (c n) -> p c n", c=N_CHUNKS)
                if lv == 0:
                    dve.tensor_copy(score[:, :, :], src).then_inc(level_read, 1)
                else:
                    dve.wait_ge(level_read, g * LEVELS + lv)
                    mask = masks[:, lv, :].unsqueeze(1).to_broadcast([P, N_CHUNKS, P])
                    dve.copy_predicated(score[:, :, :], mask, src).then_inc(level_read, 1)

            def copy_meta_levels(g):
                dve.wait_ge(level_done, g * LEVELS + META_LEVELS)
                w = step(dve.tensor_copy(score_meta[:, :], meta[0:N_META, 0:N_META]))
                for lv in range(1, META_LEVELS):
                    after(w)
                    ins = dve.copy_predicated(score_meta[:, :], masks[0:N_META, lv, 0:N_META],
                                              meta[0:N_META, lv * N_META:(lv + 1) * N_META])
                    if lv < META_LEVELS - 1:
                        w = step(ins)
                    else:
                        ins.then_inc(meta_read, 1)

            last_decay = {}

            def level_products(g, c, lv):
                m = 2 ** (lv - 1)
                qkk_c, dst = qkk[:, c % 2, :, :], qk_dec[:, lv % 2, :, :]
                if lv == 1:
                    dve.wait_ge(decay_set, 4 * (g + 1))
                if lv >= 2:
                    dve.wait_ge(level_done, g * LEVELS + lv - 1)
                    after(last_decay["second"])
                step(dve.tensor_tensor(block_half(dst, m, 1), block_half(qkk_c[:, 0:3:2, :], m, 1),
                                       block_half(decay[:, 0:2, :], m, 1), ALU.mult))
                if lv >= 2:
                    after(last_decay["first"])
                dve.tensor_tensor(block_half(dst, m, 0), block_half(qkk_c[:, 0:2, :], m, 0),
                                  block_half(decay[:, 2:4, :], m, 0), ALU.mult).then_inc(qk_ready, 1)
                if lv >= 2:
                    after(last_decay["totals"])
                first = 0 if m < N_META else N_META
                n_pairs = (T - first) // (2 * m)
                out_at = TOTALS_AT[2 * m]
                last_decay["totals"] = step(dve.tensor_tensor(
                    totals[:, :, out_at:out_at + n_pairs],
                    block_totals(slice(0, 3), m, 0), block_totals(slice(0, 3), m, 1), ALU.mult))

                def spread(a, half):
                    t = block_totals(a, m, half)
                    return t.unsqueeze(3).to_broadcast([P, 2, n_pairs, m])

                second = block_half(decay[:, 0:2, :], m, 1)
                last_decay["second"] = step(dve.tensor_tensor(second, second, spread(slice(0, 2), 0), ALU.mult))
                firsts = block_half(decay[:, 2:4, :], m, 0)
                last_decay["first"] = step(dve.tensor_tensor(firsts, firsts, spread(slice(1, 3), 1), ALU.mult))

            def chain_states(g):
                dve.wait_ge(kv_done, 2 * g + 1)
                wb = step(dve.tensor_copy(state_b[:, 3, :], pair[:, 0, 3 * P:4 * P]))
                dve.wait_ge(kv_done, 2 * g + 2)
                wf = step(dve.tensor_copy(state_f[:, 0, :], pair[:, 1, 0:P]))
                at = TOTALS_AT[P]
                for j in range(3):
                    r = 2 - j
                    after(wb)
                    wb = step(dve.scalar_tensor_tensor(state_b[:, r, :], state_b[:, r + 1, :],
                                                       totals[:, 1, at + r:at + r + 1],
                                                       pair[:, 0, r * P:(r + 1) * P], ALU.mult, ALU.add))
                    after(wf)
                    ins = dve.scalar_tensor_tensor(state_f[:, j + 1, :], state_f[:, j, :],
                                                   totals[:, 0, at + j:at + j + 1],
                                                   pair[:, 1, (j + 1) * P:(j + 2) * P], ALU.mult, ALU.add)
                    if j < 2:
                        wf = step(ins)
                    else:
                        ins.then_inc(states_ready, 1)

            def finish_head(l, c):
                n = l * HEADS + c
                w = inverse_rms(l * (HEADS + 1) + c + 2)
                gain = g_hg[:, l:l + 1] if c < HG_HEADS else g_at[:, l:l + 1]
                after(w)
                w = step(dve.scalar_tensor_tensor(o_t[:, :], o_t[:, :], gain, sq[:, :], ALU.mult, ALU.mult))
                after(w)
                dve.wait_ge(stage_read, 3 * n + 3)
                dve.tensor_tensor(o_t[:, :], o_t[:, :], gates[:, c % 2, :], ALU.mult).then_inc(mixed, 1)

            def hgrn(l, c, s):
                g = l * HG_HEADS + c
                if s == 1:
                    dve.wait_ge(stage_read, 3 * (l * HEADS + c) + 2)
                    dve.tensor_tensor(qk_dec[:, 0, 1, :], qkk[:, c % 2, 1, :], qkk[:, c % 2, 2, :],
                                      ALU.add).then_inc(qk_ready, 1)
                elif 1 < s <= LEVELS:
                    level_products(g, c, s - 1)
                    copy_level(g, s - 2)
                    if s - 2 == META_LEVELS:
                        copy_meta_levels(g)
                elif s == LEVELS + 1:
                    after(last_decay["first"])
                    dve.tensor_tensor(qk_dec[:, 0, :, :], qkk[:, c % 2, 0:3:2, :], decay[:, 0:2, :],
                                      ALU.mult).then_inc(qk_ready, 1)
                    copy_level(g, LEVELS - 1)
                    dve.tensor_tensor(qk_dec[:, 1, :, :], qkk[:, c % 2, 0:2, :], decay[:, 2:4, :],
                                      ALU.mult).then_inc(qk_ready, 1)
                elif s == LEVELS + 2:
                    chain_states(g)

            def row_max(a, i, comp):
                rows = P if i < 4 else N_META
                dve.wait_ge(s_done, a * 10 + 2 * i + comp + 1)
                dve.tensor_reduce(neg_max[0:rows, i % 2, comp:comp + 1], pair[0:rows, :, both],
                                  axis=mybir.AxisListType.XY, op=ALU.max, negate=True)\
                    .then_inc(max_ready, 1)

            def attend(l, c, s):
                a = l * AT_HEADS + c - HG_HEADS
                i, comp = s // 2, s % 2
                if i < 5:
                    row_max(a, i, comp)
                if comp == 0 and 1 <= i < 6:
                    j = i - 1
                    r = slice(0, P if j < 4 else N_META)
                    dve.wait_ge(exp_done, a * 10 + 2 * j + 2)
                    w = step(dve.reciprocal(row_inv[r, j % 2, :], row_sum[r, j % 2, :]))
                    after(w)
                    w = step(dve.tensor_scalar(row_inv[r, j % 2, 1:2], row_inv[r, j % 2, 1:2],
                                               lam[r, l:l + 1], None, ALU.mult))
                    after(w)
                    e0, e1 = decay[r, 2 * (j % 2), :], decay[r, 2 * (j % 2) + 1, :]
                    w = step(dve.tensor_scalar(e1, e1, row_inv[r, j % 2, 1:2], None, ALU.mult))
                    if j >= 2:
                        dve.wait_ge(p_turned, a * 5 + j - 1)
                    after(w)
                    dve.scalar_tensor_tensor(qk_dec[r, j % 2, 0, :], e0, row_inv[r, j % 2, 0:1], e1,
                                             ALU.mult, ALU.subtract).then_inc(p_ready, 1)

            prepare = True
            for l in range(DEPTH):
                if prepare:
                    dve.wait_ge(x_in, 16 * (KT + 1))
                    w = step(dve.tensor_scalar(g_in[:, :, :], g_in[:, :, :], math.sqrt(D_MODEL), None,
                                               ALU.mult))
                    after(w)
                norm_u(l)
                if prepare:
                    prepare_lower_bounds()
                    prepare = False
                for i in range(len(HG_TILES)):
                    follow(l, i)
                for c in range(HEADS):
                    for s in range(steps_of(c)):
                        (hgrn if c < HG_HEADS else attend)(l, c, s)
                        for i in units_after(c, s):
                            follow(l, i)
                    for i in units_after(c, steps_of(c)):
                        follow(l, i)
                    finish_head(l, c)
                for i in range(OUT_B, LAYER_UNITS):
                    follow(l, i)
            norm_out()

        @block.tensor
        def _(pe):
            def piece(l, i, k):
                what, c, j = UNITS[i]
                t = l * LAYER_UNITS + i
                if k == 0:
                    pe.wait_ge(lo_cut, t + 1)
                    if t >= 2:
                        pe.wait_ge(evacuated[t % 2], evac_count(t - 2))
                    if what == "outA":
                        pe.wait_ge(mix_lo_ready, l * HEADS + HG_HEADS)
                    if what == "outB":
                        pe.wait_ge(mix_lo_ready, (l + 1) * HEADS)
                if i == 0:
                    pe.wait_ge(u_lo_ready, l * KT + k + 1)
                hi, lo = (mix_hi, mix_lo) if what in ("outA", "outB") else (u_hi, u_lo)
                wh, wl = w_hi[:, t % N_CUT, k, :], w_lo[:, t % N_CUT, k, :]
                for w, x, p in ((wh, hi, 0), (wh, lo, 1), (wl, hi, 2)):
                    for n, cols_n in enumerate(halves):
                        ins = pe.matmul(proj[t % 2][:, n, both], w, x[:, k, cols_n],
                                        start=(k == 0 and p == 0), stop=(k == KT - 1 and p == 2))
                if k == KT - 1:
                    ins.then_inc(unit_done, 1)

            def feed(l, c, s):
                first, _ = fed_units(c)
                for q in range(pieces_by(c, s - 1), pieces_by(c, s)):
                    piece(l, first + q // KT, q % KT)

            def sum_squares(n, k):
                if n == 0 and k == 0:
                    pe.wait_ge(ones_set, 3)
                pe.wait_ge(h_sq, n * KT + k + 1)
                for b, cols_n in enumerate(halves):
                    ins = pe.matmul(pair[:, b, both], ones[:, :], decay[:, k % 4, cols_n],
                                    start=(k == 0), stop=(k == KT - 1))
                ins.then_inc(h_sq_summed, 1)

            def turn_v(l, c):
                if l == 0 and c == 0:
                    pe.wait_ge(consts_in, 16 * 8)
                t = l * LAYER_UNITS + FIRST_UNIT[c] + (3 if c < HG_HEADS else 2)
                pe.wait_ge(evacuated[t % 2], evac_count(t))
                for j in range(N_CHUNKS):
                    pe.transpose(main[:, j * P:(j + 1) * P], v_t[:, chunk(j)], ident[:, :])
                pe.transpose(meta[0:N_META, 0:P], v_t[:, 0:N_META], ident[:, :]).then_inc(v_turned, 1)

            def level(g, c, lv):
                pe.wait_ge(qk_ready, g * 10 + lv + 1)
                if lv >= 2:
                    pe.wait_ge(level_read, g * LEVELS + lv - 1)
                q = qkk[:, c % 2, 0, :] if lv == 0 else qk_dec[:, lv % 2, 0, :]
                k = qk_dec[:, lv % 2, 1, :]
                if lv < META_LEVELS:
                    pe.matmul(meta[0:N_META, lv * N_META:(lv + 1) * N_META], k[:, 0:N_META],
                              q[:, 0:N_META], start=True, stop=True)
                for j in range(N_CHUNKS):
                    ins = pe.matmul(pair[:, lv % 2, j * P:(j + 1) * P], k[:, chunk(j)], q[:, chunk(j)],
                                    start=True, stop=True)
                ins.then_inc(level_done, 1)

            def sum_head_squares(n):
                pe.wait_ge(sq_ready, n + 1)
                for b, cols_n in enumerate(halves):
                    ins = pe.matmul(pair[:, b, both], ones[:, :], sq[:, cols_n], start=True, stop=True)
                ins.then_inc(sq_summed, 1)

            def hgrn(l, c, s):
                n, g = l * HEADS + c, l * HG_HEADS + c
                if s == 0:
                    turn_v(l, c)
                elif s <= LEVELS:
                    if s == 1:
                        pe.wait_ge(v_ready, n + 1)
                        if n > 0:
                            pe.wait_ge(mixed, n)
                    level(g, c, s - 1)
                elif s == LEVELS + 1:
                    pe.wait_ge(qk_ready, g * 10 + 9)
                    pe.wait_ge(level_read, g * LEVELS + 7)
                    for j in range(N_CHUNKS):
                        ins = pe.transpose(pair[:, 0, j * P:(j + 1) * P], qk_dec[:, 0, 1, chunk(j)],
                                           ident[:, :])
                    ins.then_inc(k_turned, 1)
                    pe.wait_ge(qk_ready, g * 10 + 10)
                    pe.wait_ge(level_read, g * LEVELS + 8)
                    pe.wait_ge(meta_read, g + 1)
                    for j in range(N_CHUNKS - 1):
                        pe.transpose(pair[:, 1, j * P:(j + 1) * P], qk_dec[:, 1, 1, chunk(j)], ident[:, :])
                    pe.transpose(meta[0:N_META, 0:P], qk_dec[:, 1, 1, 0:N_META], ident[:, :])\
                        .then_inc(k_turned, 1)
                elif s == LEVELS + 2:
                    pe.wait_ge(k_ready, 2 * g + 1)
                    for j in range(N_CHUNKS):
                        ins = pe.matmul(pair[:, 0, j * P:(j + 1) * P], cols[:, j, :], v_main[:, j, :],
                                        start=True, stop=True)
                    ins.then_inc(kv_done, 1)
                    pe.wait_ge(k_ready, 2 * g + 2)
                    pe.matmul(pair[:, 1, 0:P], cols[0:N_META, 7, :], v_meta[:, :], start=True, stop=True)
                    for j in range(N_CHUNKS - 1):
                        ins = pe.matmul(pair[:, 1, (j + 1) * P:(j + 2) * P], cols[:, 4 + j, :],
                                        v_main[:, j, :], start=True, stop=True)
                    ins.then_inc(kv_done, 1)
                elif s == LEVELS + 3:
                    pe.wait_ge(states_ready, g + 1)
                    for j in range(N_CHUNKS):
                        out = main[:, j * P:(j + 1) * P]
                        pe.matmul(out, v_main[:, j, :], score[:, j, :], start=True, stop=False)
                        pe.matmul(out, state_f[:, j, :], qk_dec[:, 0, 0, chunk(j)], start=False,
                                  stop=(j == 3))
                        if j < 3:
                            pe.matmul(out, state_b[:, j + 1, :], qk_dec[:, 1, 0, chunk(j)],
                                      start=False, stop=True)
                    out = meta[:, 0:N_META]
                    pe.matmul(out, v_meta[:, :], score_meta[:, :], start=True, stop=False)
                    pe.matmul(out, state_b[:, 0, :], qk_dec[:, 1, 0, 0:N_META], start=False, stop=True)\
                        .then_inc(o_done, 1)
                else:
                    sum_head_squares(n)

            def attend(l, c, s):
                n, a = l * HEADS + c, l * AT_HEADS + c - HG_HEADS
                i, comp = s // 2, s % 2
                if s == 0:
                    turn_v(l, c)
                    pe.wait_ge(stage_read, 3 * n + 2)
                    pe.wait_ge(mixed, n)
                if i < 5:
                    rows = P if i < 4 else N_META
                    cs = chunk(i) if i < 4 else slice(0, N_META)
                    part = slice(comp * AT_HEAD_DIM, (comp + 1) * AT_HEAD_DIM)
                    if s > 0:
                        pe.wait_ge(exp_done, a * 10 + s)
                    for b, keys in enumerate(halves):
                        ins = pe.matmul(pair[0:rows, b, both], qkk[part, c % 2, 0, cs],
                                        qkk[part, c % 2, 1, keys], start=True, stop=True)
                    ins.then_inc(s_done, 1)
                if comp == 0 and 2 <= i < 7:
                    j = i - 2
                    rows = P if j < 4 else N_META
                    pe.wait_ge(pt_ready, a * 5 + j + 1)
                    for kk in range(4):
                        pe.matmul(meta[:, 0:rows], v_main[:, kk, :], cols[:, kk, 0:rows],
                                  start=(kk == 0), stop=False)
                    pe.matmul(meta[:, 0:rows], v_meta[:, :], cols[0:N_META, 4, 0:rows],
                              start=False, stop=True).then_inc(pv_done, 1)
                if comp == 1 and 1 <= i < 6:
                    j = i - 1
                    rows = P if j < 4 else N_META
                    if j == 0:
                        pe.wait_ge(v_ready, n + 1)
                    else:
                        pe.wait_ge(pv_read, a * 5 + j)
                    pe.wait_ge(p_ready, a * 5 + j + 1)
                    p = qk_dec[0:rows, j % 2, 0, :]
                    for kk in range(4):
                        pe.transpose(main[:, kk * P:kk * P + rows], p[:, chunk(kk)], ident[0:rows, 0:rows])
                    pe.transpose(meta[0:N_META, 0:rows], p[:, 0:N_META], ident[0:rows, 0:rows])\
                        .then_inc(p_turned, 1)
                if s == AT_STEPS - 1:
                    sum_head_squares(n)

            for k in range(KT):
                sum_squares(0, k)
            for l in range(DEPTH):
                for i in range(len(HG_TILES)):
                    for k in range(KT):
                        piece(l, i, k)
                for c in range(HEADS):
                    for s in range(steps_of(c)):
                        (hgrn if c < HG_HEADS else attend)(l, c, s)
                        feed(l, c, s)
                for j in range(OUT_TILES):
                    for k in range(KT):
                        piece(l, OUT_B + j, k)
                    if j > 0:
                        sum_squares(l + 1, j - 1)
                sum_squares(l + 1, OUT_TILES - 1)


def packed_weights(w_in, w_out):
    units = np.empty((DEPTH * LAYER_UNITS, P, KT, P), w_in.dtype)
    turn = np.arange(P).reshape(2, 2, 32).transpose(0, 2, 1).reshape(P)
    group = {"q": 0, "zf": 1, "zb": 2, "v": 3, "g": 4, "aq": 5, "ak": 6, "av": 7, "ag": 8}
    for l in range(DEPTH):
        for i, (what, c, j) in enumerate(UNITS):
            if what in ("outA", "outB"):
                rows = slice(0, D_MODEL) if what == "outA" else slice(D_MODEL, 2 * D_MODEL)
                tile = w_out[l][rows, j * P:(j + 1) * P]
            else:
                at = group[what] * D_MODEL + (c % HG_HEADS) * P
                tile = w_in[l][:, at:at + P]
                if what in ("aq", "ak"):
                    tile = tile[:, turn]
            units[l * LAYER_UNITS + i] = tile.reshape(KT, P, P).transpose(1, 0, 2)
    return units


def constants():
    s, t = np.meshgrid(np.arange(P), np.arange(P), indexing="ij")
    level = np.zeros((P, P), np.int64)
    for lv in range(1, LEVELS):
        level[(s ^ t) >= 2 ** (lv - 1)] = lv
    masks = np.stack([(level == lv) for lv in range(LEVELS)], axis=1).astype(np.int32)
    inv = np.float32(ROPE_THETA) ** (-np.arange(0, AT_HEAD_DIM, 2, dtype=np.float32) / np.float32(AT_HEAD_DIM))
    ang = np.arange(T, dtype=np.float32)[None, :] * inv.astype(np.float32)[:, None]
    rope = np.empty((P, 2, T), np.float32)
    row = np.arange(P)
    pair = (row % AT_HEAD_DIM) // 2
    rope[:, 0] = np.cos(ang)[pair]
    rope[:, 1] = np.sin(ang)[pair] * np.where(row % 2 == 0, -1.0, 1.0)[:, None]
    return masks, np.eye(P, dtype=np.float32), rope


def kernel(x, meta_tokens, norm_g, w_in, hg_lb_logits, hg_norm_g, diff_lambda, diff_subln_g,
           w_out, final_norm_g):
    import concourse.bacc as bacc
    from concourse.bass_utils import run_bass_kernel_spmd

    x, meta_tokens, norm_g, w_in, w_out = (np.asarray(a) for a in (x, meta_tokens, norm_g, w_in, w_out))
    hg_lb_logits, hg_norm_g, diff_lambda, diff_subln_g, final_norm_g = (
        np.asarray(a) for a in (hg_lb_logits, hg_norm_g, diff_lambda, diff_subln_g, final_norm_g))
    tokens = np.concatenate([meta_tokens, x[0]], axis=0)
    masks, identity, rope = constants()
    arrays = {
        "x_t": tokens.T.reshape(KT, P, T).transpose(1, 0, 2),
        "w_units": packed_weights(w_in, w_out),
        "norm_g": norm_g.reshape(DEPTH, KT, P).transpose(2, 0, 1),
        "lb_logits": hg_lb_logits.reshape(DEPTH, 2 * HG_HEADS, P).transpose(2, 0, 1),
        "hg_gain": hg_norm_g.T,
        "lambdas": np.broadcast_to(diff_lambda.reshape(1, DEPTH * 2, 2, AT_HEAD_DIM),
                                   (P, DEPTH * 2, 2, AT_HEAD_DIM)),
        "at_gain": diff_subln_g.T,
        "final_g": final_norm_g.reshape(KT, P).T,
        "level_masks": masks,
        "identity": identity,
        "rope": rope,
    }
    arrays = {k: np.ascontiguousarray(v) for k, v in arrays.items()}
    nc = bacc.Bacc("TRN2", target_bir_lowering=False, num_devices=1)
    args = [nc.dram_tensor(k, v.shape, mybir.dt.from_np(v.dtype), kind="ExternalInput").ap()
            for k, v in arrays.items()]
    out = nc.dram_tensor("out_t", (KT, P, SEQ), mybir.dt.float32, kind="ExternalOutput").ap()
    encoder_trunk(nc, *args, out)
    r = run_bass_kernel_spmd(nc, [arrays], core_ids=[0])
    return r.results[0]["out_t"].reshape(D_MODEL, SEQ).T.reshape(1, SEQ, D_MODEL)
```

```python
import math
from contextlib import ExitStack

import concourse.bass as bass
import numpy as np
from concourse import mybir

P = 128
DEPTH = 2
D_MODEL = 1024
N_META = 16
SEQ = 512
T = N_META + SEQ
HALF = T // 2
HG_HEADS = 8
AT_HEADS = 8
AT_HEAD_DIM = 64
HEADS = HG_HEADS + AT_HEADS
KT = D_MODEL // P
IN_TILES = 9216 // P
OUT_TILES = D_MODEL // P
NORM_EPS = 1e-6
F_FLOOR = 1e-30
ROPE_THETA = 10000.0
N_CHUNKS = SEQ // P
LEVELS = 8
META_LEVELS = 5
HG_TILES = ("zf", "zb", "q", "v", "g")
AT_TILES = ("aq", "ak", "av", "ag")
STAGE_USE = {"zf": 0, "zb": 1, "g": 2, "aq": 0, "ak": 1, "ag": 2}

TOTALS_AT = {}
_at = 0
for _m in (2, 4, 8, 16, 32, 64, 128):
    TOTALS_AT[_m] = _at
    _at += T // _m
TOTALS = _at


def layer_units():
    units = []
    for c in range(HEADS):
        units += [(what, c, i, c - 1) for i, what in enumerate(HG_TILES if c < HG_HEADS else AT_TILES)]
        if c == HG_HEADS + 1:
            units += [("outA", c, j, c - 1) for j in range(OUT_TILES)]
    return units + [("outB", HEADS, j, HEADS - 1) for j in range(OUT_TILES)]


UNITS = layer_units()
LAYER_UNITS = len(UNITS)
FIRST_UNIT = {c: next(i for i, u in enumerate(UNITS) if u[1] == c and u[0] != "outA") for c in range(HEADS)}
OUT_A_END = max(i for i, u in enumerate(UNITS) if u[0] == "outA") + 1
OUT_B = LAYER_UNITS - OUT_TILES

TURN_KEYS = LEVELS + 1
HG_STEPS = LEVELS + 5
AT_STEPS = 2 * 6 + 1
DECAY_STEP = TURN_KEYS + 1
STACK_STEP = 2 * 5 - 1
HG_FEED = (2, 3, 3, 3, 3, 3, 4, 4, 3, 3, 3, 4, 2)
AT_FEED = (3, 3, 3, 2, 2, 3, 2, 3, 2, 3, 2, 2, 2)
EARLY_K = KT - 1
EARLY_FED = EARLY_K + 4


STACK_AFTER = {FIRST_UNIT[c] + (12 if c == HG_HEADS + 1 else 6): c - HG_HEADS for c in range(HG_HEADS, HEADS)}


def steps_of(c):
    return HG_STEPS if c < HG_HEADS else AT_STEPS


def mix_step(c):
    return HG_STEPS - 2 if c < HG_HEADS else 3


def share_fed(c, s):
    shares = HG_FEED if c < HG_HEADS else AT_FEED
    return sum(shares[:s + 1]) / sum(shares)


def fed_units(c):
    fed = [i for i, u in enumerate(UNITS) if u[3] == c]
    return fed[0], fed[-1] + 1


def pieces_by(c, s):
    if s < 0:
        return 0
    first, last = fed_units(c)
    pieces = EARLY_FED if c == HEADS - 1 else (last - first) * KT
    return round(share_fed(c, s) * pieces)


def units_after(c, s):
    first, _ = fed_units(c)
    if c == HEADS - 1:
        return range(0)
    return range(first + pieces_by(c, s - 2) // KT, first + pieces_by(c, s - 1) // KT)


def units_left(c):
    return units_after(c, steps_of(c)) if c >= 0 else ()


def units_followed(c, s):
    def spread_out(c):
        return c > HG_HEADS

    last = steps_of(c) - 1
    if not spread_out(c):
        units = [*units_after(c, s)]
    elif s % 2 == 1:
        units = [*units_after(c, s - 2), *units_after(c, s - 1)]
    else:
        units = []
    if s == 1 and c > 0:
        end = steps_of(c - 1)
        late = [i for t in (end - 2, end - 1) for i in units_after(c - 1, t)] if spread_out(c - 1) else []
        units = [*late, *units_left(c - 1), *units]
    return units


def encoder_trunk(nc, x_t, w_units, norm_g, lb_logits, hg_gain, lambdas, at_gain, final_g,
                  level_masks, identity, rope, out_t):
    f32 = mybir.dt.float32
    f32r = mybir.dt.float32r
    i32 = mybir.dt.int32
    ALU = mybir.AluOpType
    ACT = mybir.ActivationFunctionType
    X = mybir.AxisListType.X

    N_RAW = 2
    N_CUT = 3

    ctx = ExitStack()
    with ctx:
        def sb(name, shape, dt=f32):
            return ctx.enter_context(nc.sbuf_tensor(name, shape, dt))

        def sem(name):
            return ctx.enter_context(nc.semaphore(name))

        h = sb("h", [P, KT, T])
        u_hi = sb("u_hi", [P, KT, T], f32r)
        u_lo = sb("u_lo", [P, KT, T], f32r)
        mix_hi = sb("mix_hi", [P, 8, T], f32r)
        mix_lo = sb("mix_lo", [P, 8, T], f32r)
        w_raw = sb("w_raw", [P, N_RAW, KT, P])
        w_hi = sb("w_hi", [P, N_CUT, KT, P], f32r)
        w_lo = sb("w_lo", [P, N_CUT, KT, P], f32r)
        masks = sb("masks", [P, LEVELS - 1, P], i32)
        ident = sb("ident", [P, P])
        ones = sb("ones", [P, P])
        cos_sin = sb("cos_sin", [P, 2, T])
        g_in = sb("g_in", [P, DEPTH, KT])
        g_final = sb("g_final", [P, KT])
        g_hg = sb("g_hg", [P, DEPTH])
        g_at = sb("g_at", [P, DEPTH])
        lb = sb("lb", [P, DEPTH, 2 * HG_HEADS])
        one_minus_lb = sb("one_minus_lb", [P, DEPTH, 2 * HG_HEADS])
        lb_work = sb("lb_work", [P, 4, 2 * HG_HEADS])
        lam_sum = sb("lam_sum", [P, DEPTH, 2])
        lam = sb("lam", [P, DEPTH])
        stage = sb("stage", [P, 2, 2, T])
        gate_f = sb("gate_f", [P, 3, T])
        totals = sb("totals", [P, 3, TOTALS])
        decay = sb("decay", [P, 4, T])
        qkk = sb("qkk", [P, 2, 3, T])
        qk_dec = sb("qk_dec", [P, 2, 2, T])
        q_stack = sb("q_stack", [P, 2, T], f32r)
        k_stack = sb("k_stack", [P, 2, T], f32r)
        k_low = sb("k_low", [P, T], f32r)
        gates = sb("gates", [P, 2, T])
        v_t = sb("v_t", [P, T])
        v_main = sb("v_main", [P, N_CHUNKS, P])
        v_meta = sb("v_meta", [N_META, P])
        cols = sb("cols", [P, 2 * N_CHUNKS, P])
        state_f = sb("state_f", [P, N_CHUNKS, P])
        state_b = sb("state_b", [P, N_CHUNKS, P])
        lam_in = state_f[:, :, :].rearrange("p a (b d) -> p a b d", b=2)
        lam_prod = state_b[:, 0:DEPTH, :].rearrange("p a (b d) -> p (a b) d", b=2)
        score = sb("score", [P, N_CHUNKS, P])
        score_meta = sb("score_meta", [N_META, N_META])
        o_rows = sb("o_rows", [P, N_CHUNKS + 1, P])
        o_sums = sb("o_sums", [P, N_CHUNKS + 1])
        o_inv = sb("o_inv", [P, N_CHUNKS + 1])
        minus_half = sb("minus_half", [P, N_CHUNKS + 1])
        mixed_t = sb("mixed_t", [P, T])
        sq = mixed_t
        eps_count = sb("eps_count", [P, 1])
        neg_max = sb("neg_max", [P, 2, 2])
        row_sum = sb("row_sum", [P, 2, 2])
        row_inv = sb("row_inv", [P, 2, 2])

        proj = [ctx.enter_context(nc.psum_tensor(f"proj{i}", [P, 2, 512], f32)) for i in range(2)]
        pair = ctx.enter_context(nc.psum_tensor("pair", [P, 2, 512], f32))
        main = ctx.enter_context(nc.psum_tensor("main", [P, 512], f32))
        meta = ctx.enter_context(nc.psum_tensor("meta", [P, 512], f32))

        consts_in = sem("consts_in")
        x_in = sem("x_in")
        raw_in = [sem(f"raw_in{i}") for i in range(N_RAW)]
        out_stored = sem("out_stored")
        ones_set = sem("ones_set")
        hi_cut = sem("hi_cut")
        lo_cut = sem("lo_cut")
        unit_done = sem("unit_done")
        evacuated = [sem(f"evacuated{i}") for i in range(2)]
        stage_read = sem("stage_read")
        decay_set = sem("decay_set")
        qk_ready = sem("qk_ready")
        level_done = sem("level_done")
        level_read = sem("level_read")
        meta_read = sem("meta_read")
        v_turned = sem("v_turned")
        v_ready = sem("v_ready")
        k_turned = sem("k_turned")
        k_ready = sem("k_ready")
        kv_done = sem("kv_done")
        states_ready = sem("states_ready")
        o_done = sem("o_done")
        sq_ready = sem("sq_ready")
        o_taken = sem("o_taken")
        sums_set = sem("sums_set")
        o_inv_ready = sem("o_inv_ready")
        o_scaled = sem("o_scaled")
        o_turned = sem("o_turned")
        pool_step = sem("pool_step")
        root_ready = sem("root_ready")
        mixed = sem("mixed")
        mix_hi_ready = sem("mix_hi_ready")
        mix_lo_ready = sem("mix_lo_ready")
        s_done = sem("s_done")
        max_ready = sem("max_ready")
        exp_done = sem("exp_done")
        p_ready = sem("p_ready")
        p_turned = sem("p_turned")
        pt_ready = sem("pt_ready")
        pv_done = sem("pv_done")
        pv_read = sem("pv_read")
        h_sq = sem("h_sq")
        h_sq_summed = sem("h_sq_summed")
        u_ready = sem("u_ready")
        u_hi_ready = sem("u_hi_ready")
        u_lo_ready = sem("u_lo_ready")
        out_ready = sem("out_ready")
        bounds_ready = sem("bounds_ready")
        k_scaled = sem("k_scaled")
        stack_hi = sem("stack_hi")
        stack_lo = sem("stack_lo")
        stacked = sem("stacked")
        lb_exp = sem("lb_exp")
        lb_max = sem("lb_max")
        act_step = sem("act_step")
        dve_step = sem("dve_step")

        halves = (slice(0, HALF), slice(HALF, T))
        comps = (slice(0, AT_HEAD_DIM), slice(AT_HEAD_DIM, P))
        both = slice(0, HALF)

        def chunk(c):
            return slice(N_META + c * P, N_META + (c + 1) * P)

        def evac_count(t):
            return t // 2 + 1

        def squares(j):
            return slice((j % N_CHUNKS) * P, (j % N_CHUNKS + 1) * P)

        def two(ap):
            return ap.rearrange("p (h n) -> p h n", h=2)

        def block_half(x, m, half):
            first = 0 if m < N_META else N_META
            return x[:, :, first:T].rearrange("p a (b h m) -> p a b h m", h=2, m=m)[:, :, :, half, :]

        def block_totals(a, m, half):
            n = (T if m <= N_META else SEQ) // m
            skip = 1 if m == N_META else 0
            src = gate_f[:, a, 0:T] if m == 1 else \
                totals[:, a, TOTALS_AT[m] + skip:TOTALS_AT[m] + n]
            return src.rearrange("p a (b h) -> p a b h", h=2)[:, :, :, half]

        def u_out(k):
            if k < 4:
                return decay[:, k, N_META:T]
            return qkk[:, (k - 4) // 2, (k - 4) % 2, N_META:T]

        block = ctx.enter_context(nc.Block())

        @block.sync
        def _(sp):
            def stack_other(a):
                sp.wait_ge(stack_hi, 4 * (a + 1))
                for comp, rows in enumerate(comps):
                    sp.dma_start(k_stack[comps[1 - comp], comp, :].bitcast(f32),
                                 k_stack[rows, comp, :].bitcast(f32)).then_inc(stacked, 16)
                sp.wait_ge(stack_lo, 4 * a + 2)
                for comp, rows in enumerate(comps):
                    sp.dma_start(q_stack[comps[1 - comp], comp, :].bitcast(f32), gate_f[rows, 2, :])\
                        .then_inc(stacked, 16)

            for k in range(KT):
                sp.dma_start(h[:, k, :], x_t[:, k, :]).then_inc(x_in, 16)
            sp.dma_start(g_in[:, :, :], norm_g).then_inc(x_in, 16)
            for u in range(DEPTH * LAYER_UNITS):
                if u == N_RAW:
                    for dst, src in ((ident[:, :], identity), (lb[:, :, :], lb_logits), (g_hg[:, :], hg_gain),
                                     (g_at[:, :], at_gain), (g_final[:, :], final_g),
                                     (masks[:, :, :], level_masks), (cos_sin[:, :, :], rope),
                                     (lam_in[:, :, :, :], lambdas)):
                        sp.dma_start(dst, src).then_inc(consts_in, 16)
                if u >= N_RAW:
                    sp.wait_ge(lo_cut, u - N_RAW + 1)
                sp.dma_start(w_raw[:, u % N_RAW, :, :], w_units[u]).then_inc(raw_in[u % N_RAW], 16)
                if u % LAYER_UNITS in STACK_AFTER:
                    stack_other(u // LAYER_UNITS * AT_HEADS + STACK_AFTER[u % LAYER_UNITS])
            for k in range(KT):
                sp.wait_ge(out_ready, k + 1)
                sp.dma_start(out_t[k], u_out(k)).then_inc(out_stored, 16)
            sp.wait_ge(out_stored, 16 * KT)

        @block.gpsimd
        def _(pool):
            pool.memset(ones[:, :], 1.0).then_inc(ones_set, 1)
            pool.memset(eps_count[:, :], D_MODEL * NORM_EPS).then_inc(ones_set, 1)
            pool.memset(o_sums[:, :], 0.0).then_inc(ones_set, 1)
            pool.memset(minus_half[:, :], -0.5).then_inc(ones_set, 1)

            def cut_low(u):
                pool.wait_ge(hi_cut, u + 1)
                pool.tensor_tensor(w_lo[:, u % N_CUT, :, :], w_raw[:, u % N_RAW, :, :],
                                   w_hi[:, u % N_CUT, :, :].bitcast(f32), ALU.subtract)\
                    .then_inc(lo_cut, 1)

            def set_decay(l, c):
                g = l * HG_HEADS + c
                if g > 0:
                    pool.wait_ge(qk_ready, 10 * g)
                pool.memset(decay[:, 1, :], 1.0).then_inc(decay_set, 1)
                pool.memset(decay[:, 3, :], 1.0).then_inc(decay_set, 1)

            def invert_rms(n):
                pool.wait_ge(sq_ready, n + 1)
                if n > 0:
                    pool.wait_ge(o_scaled, n)
                pool.tensor_scalar(o_inv[:, :], o_sums[:, :], P * NORM_EPS, None, ALU.add)\
                    .then_inc(pool_step, 1)
                pool.wait_ge(pool_step, n + 1)
                pool.tensor_tensor(o_inv[:, :], o_inv[:, :], minus_half[:, :], ALU.pow)\
                    .then_inc(o_inv_ready, 1)

            def cut_mixed(n):
                pool.wait_ge(mix_hi_ready, n + 1)
                pool.tensor_tensor(mix_lo[:, n % 8, :], mixed_t[:, :],
                                   mix_hi[:, n % 8, :].bitcast(f32), ALU.subtract)\
                    .then_inc(mix_lo_ready, 1)

            for u in range(N_CUT):
                cut_low(u)
            for l in range(DEPTH):
                base = l * LAYER_UNITS

                def follow(units):
                    for i in units:
                        if base + i + N_CUT < DEPTH * LAYER_UNITS:
                            cut_low(base + i + N_CUT)

                follow(range(len(HG_TILES)))
                set_decay(l, 0)
                for c in range(HEADS):
                    n = l * HEADS + c
                    for s in range(steps_of(c)):
                        if s == mix_step(c) and c > 0:
                            cut_mixed(n - 1)
                        if s == DECAY_STEP and c + 1 < HG_HEADS:
                            set_decay(l, c + 1)
                        follow(units_after(c, s))
                    invert_rms(n)
                    follow(units_left(c))
                cut_mixed(l * HEADS + HEADS - 1)
                follow(range(OUT_B, LAYER_UNITS))

        @block.scalar
        def _(act):
            own = [0]
            first_squares = [0]

            def step(ins):
                own[0] += 1
                ins.then_inc(act_step, 1)
                return own[0]

            def cut_high(u):
                act.wait_ge(raw_in[u % N_RAW], 16 * (u // N_RAW + 1))
                if u >= N_CUT:
                    act.wait_ge(unit_done, u - N_CUT + 1)
                act.activation(w_hi[:, u % N_CUT, :, :], w_raw[:, u % N_RAW, :, :], ACT.Copy)\
                    .then_inc(hi_cut, 1)

            def square_h(n, k):
                if n == 0:
                    act.wait_ge(x_in, 16 * (KT + 1))
                else:
                    t = (n - 1) * LAYER_UNITS + OUT_B + k
                    act.wait_ge(evacuated[t % 2], evac_count(t))
                if k >= 4:
                    act.wait_ge(h_sq_summed, n * KT + k - 4 + 1)
                act.activation(decay[:, k % 4, :], h[:, k, :], ACT.Square).then_inc(h_sq, 1)

            def root():
                act.activation(two(sq[:, :]), pair[:, :, both], ACT.Sqrt, bias=eps_count[:, :])\
                    .then_inc(root_ready, 1)

            def set_decay(l, c):
                g = l * HG_HEADS + c
                act.wait_ge(stage_read, 3 * (l * HEADS + c) + 2)
                if g > 0:
                    act.wait_ge(qk_ready, 10 * g)
                act.activation(decay[:, 0:4:2, :], gate_f[:, 0:2, :], ACT.Copy).then_inc(decay_set, 1)
                act.activation(gate_f[:, 2, :], gate_f[:, 0, :], ACT.Copy).then_inc(decay_set, 1)

            def cut_u(l):
                act.wait_ge(h_sq_summed, (l + 1) * KT)
                root()
                if l == DEPTH:
                    return
                for k in range(KT):
                    act.wait_ge(u_ready, l * KT + k + 1)
                    act.activation(u_hi[:, k, :], qk_dec[:, (k % 4) // 2, k % 2, :], ACT.Copy)\
                        .then_inc(u_hi_ready, 1)

            def evacuate(l, i):
                what, c, j, _ = UNITS[i]
                t = l * LAYER_UNITS + i
                src = proj[t % 2][:, :, both]
                if what in ("outA", "outB"):
                    act.wait_ge(unit_done, t + 1)
                else:
                    act.wait_ge(unit_done, t + 1)
                    use = (l * HEADS + c) * 3 + STAGE_USE.get(what, 0)
                    if what in HG_TILES and l * HG_HEADS + c > 0:
                        act.wait_ge(k_scaled, 2 * (l * HG_HEADS + c))
                    if what not in ("q", "v", "av") and use >= 2:
                        act.wait_ge(stage_read, use - 1)
                    a, b = two(stage[:, use % 2, 0, :]), two(stage[:, use % 2, 1, :])
                    done = evacuated[t % 2]
                    if what in ("zf", "zb"):
                        d = 0 if what == "zf" else 1
                        row = d * HG_HEADS + c
                        if t == 0:
                            act.wait_ge(bounds_ready, 1)
                        step(act.activation(a, src, ACT.Sigmoid))
                        act.activation(b, src, ACT.Sigmoid, scale=-1.0).then_inc(done, 1)
                        act.wait_ge(done, evac_count(t))
                        act.activation(qkk[:, c % 2, 1 + d, :], stage[:, use % 2, 1, :], ACT.Copy,
                                       scale=one_minus_lb[:, l, row:row + 1]).then_inc(k_scaled, 1)
                    elif what == "q":
                        act.activation(two(qkk[:, c % 2, 0, :]), src, ACT.Copy).then_inc(done, 1)
                    elif what in ("v", "av"):
                        act.activation(two(v_t[:, :]), src, ACT.Copy).then_inc(done, 1)
                    elif what in ("g", "ag"):
                        if what == "g":
                            step(act.activation(a, src, ACT.Sigmoid))
                        else:
                            step(act.activation(a, src, ACT.Tanh, scale=0.5))
                        act.activation(b, src, ACT.Copy).then_inc(done, 1)
                    else:
                        act.activation(a, src, ACT.Copy,
                                       scale=AT_HEAD_DIM ** -0.5 if what == "aq" else 1.0)\
                            .then_inc(done, 1)
                if t + N_CUT < DEPTH * LAYER_UNITS:
                    cut_high(t + N_CUT)

            def copy_v(n):
                act.wait_ge(v_turned, n + 1)
                step(act.activation(v_main[:, :, :], main[:, :].rearrange("p (c n) -> p c n", c=4), ACT.Copy))
                act.activation(v_meta[:, :], meta[0:N_META, 0:P], ACT.Copy).then_inc(v_ready, 1)

            def scale_output(n):
                act.wait_ge(o_inv_ready, n + 1)
                for j in range(N_CHUNKS + 1):
                    rows = P if j < N_CHUNKS else N_META
                    ins = act.activation(o_rows[0:rows, j, :], o_rows[0:rows, j, :], ACT.Copy,
                                         scale=o_inv[0:rows, j:j + 1])
                    if j < N_CHUNKS:
                        step(ins)
                    else:
                        ins.then_inc(o_scaled, 1)

            def copy_diagonal(g):
                act.wait_ge(level_done, g * LEVELS + 1)
                act.activation(score[:, :, :], pair[:, 0, :].rearrange("p (c n) -> p c n", c=N_CHUNKS),
                               ACT.Copy).then_inc(level_read, 1)

            def hgrn(l, c, s):
                n, g = l * HEADS + c, l * HG_HEADS + c
                if s == 1:
                    copy_diagonal(g)
                if s == 2 and c > 0:
                    scale_output(n - 1)
                if s == TURN_KEYS:
                    copy_v(n)
                    act.wait_ge(k_turned, 2 * g + 1)
                    act.activation(cols[:, 0:4, :], pair[:, 0, :].rearrange("p (c n) -> p c n", c=4),
                                   ACT.Copy).then_inc(k_ready, 1)
                if s == TURN_KEYS + 1:
                    act.wait_ge(k_turned, 2 * g + 2)
                    step(act.activation(cols[:, 4:7, :],
                                        pair[:, 1, 0:3 * P].rearrange("p (c n) -> p c n", c=3), ACT.Copy))
                    act.activation(cols[0:N_META, 7, :], meta[0:N_META, 0:P], ACT.Copy)\
                        .then_inc(k_ready, 1)
                if s == HG_STEPS - 1:
                    if n > 0:
                        act.wait_ge(o_turned, 2 * n)
                    act.wait_ge(o_done, g + 1)
                    step(act.activation(o_rows[:, 0:N_CHUNKS, :],
                                        main[:, :].rearrange("p (c n) -> p c n", c=4), ACT.Copy))
                    act.activation(o_rows[0:N_META, N_CHUNKS, :], meta[0:N_META, 0:P], ACT.Copy)\
                        .then_inc(o_taken, 1)
                    act.wait_ge(o_taken, n + 1)
                    for j in range(N_CHUNKS + 1):
                        rows = P if j < N_CHUNKS else N_META
                        ins = act.activation(cols[0:rows, j, :], o_rows[0:rows, j, :], ACT.Square,
                                             accum_out=o_sums[0:rows, j:j + 1])
                        if j < N_CHUNKS:
                            step(ins)
                        else:
                            ins.then_inc(sq_ready, 1)

            def attend(l, c, s):
                n, a = l * HEADS + c, l * AT_HEADS + c - HG_HEADS
                i, comp = s // 2, s % 2
                if i < 5:
                    rows = P if i < 4 else N_META
                    if comp == 0 and i >= 2:
                        act.wait_ge(p_ready, a * 5 + i - 1)
                    act.wait_ge(max_ready, a * 10 + 2 * i + comp + 1)
                    act.activation(two(decay[0:rows, 2 * (i % 2) + comp, :]), pair[0:rows, :, both],
                                   ACT.Exp, bias=neg_max[0:rows, i % 2, comp:comp + 1],
                                   accum_out=row_sum[0:rows, i % 2, comp:comp + 1]).then_inc(exp_done, 1)
                if s == 1:
                    copy_v(n)
                if comp == 0 and 2 <= i < 7:
                    j = i - 2
                    rows = P if j < 4 else N_META
                    if j == 0:
                        act.wait_ge(o_turned, 2 * n)
                        act.wait_ge(mix_lo_ready, n)
                    act.wait_ge(pv_done, a * 5 + j + 1)
                    inv = row_inv[0:rows, j % 2, 0:1]
                    act.activation(o_rows[0:rows, j, :], meta[0:rows, 0:P], ACT.Copy, scale=inv)\
                        .then_inc(pv_read if j < 4 else o_taken, 1)
                    if j < 4:
                        act.wait_ge(pv_read, a * 4 + j + 1)
                    else:
                        act.wait_ge(o_taken, n + 1)
                        act.wait_ge(act_step, first_squares[0])
                    act.activation(sq[0:rows, squares(j)], o_rows[0:rows, j, :], ACT.Square,
                                   accum_out=o_sums[0:rows, j:j + 1]).then_inc(act_step if j < 4 else sq_ready, 1)
                    if j < 4:
                        own[0] += 1
                    if j == 0:
                        first_squares[0] = own[0]
                if comp == 1 and 1 <= i < 6:
                    j = i - 1
                    rows = P if j < 4 else N_META
                    act.wait_ge(p_turned, a * 5 + j + 1)
                    step(act.activation(cols[:, 0:4, 0:rows],
                                        main[:, :].rearrange("p (c n) -> p c n", c=4)[:, :, 0:rows],
                                        ACT.Copy))
                    act.activation(cols[0:N_META, 4, 0:rows], meta[0:N_META, 0:rows], ACT.Copy)\
                        .then_inc(pt_ready, 1)

            def stack_high(l, c):
                a = l * AT_HEADS + c - HG_HEADS
                act.wait_ge(stage_read, 3 * (l * HEADS + c) + 2)
                for i, stack in enumerate((q_stack, k_stack)):
                    for comp, rows in enumerate(comps):
                        act.activation(stack[rows, comp, :], gate_f[rows, i, :], ACT.Copy)\
                            .then_inc(stack_hi, 1)

            def round_mixed(l, c):
                n = l * HEADS + c
                if c >= HG_HEADS:
                    act.wait_ge(unit_done, l * LAYER_UNITS + OUT_A_END)
                act.wait_ge(mixed, n + 1)
                act.activation(mix_hi[:, c % 8, :], mixed_t[:, :], ACT.Copy).then_inc(mix_hi_ready, 1)

            act.wait_ge(ones_set, 4)
            for u in range(N_RAW):
                cut_high(u)
            for k in range(KT):
                square_h(0, k)
            for u in range(N_RAW, N_CUT):
                cut_high(u)
            for l in range(DEPTH):
                cut_u(l)
                if l == 0:
                    act.wait_ge(lb_max, 1)
                    act.activation(lb_work[:, 0:2, :], lb_work[:, 0:2, :], ACT.Exp).then_inc(lb_exp, 1)
                    act.wait_ge(lb_max, 2)
                    act.activation(lam_sum[:, :, :], lam_sum[:, :, :], ACT.Exp).then_inc(lb_exp, 1)
                for i in range(len(HG_TILES)):
                    evacuate(l, i)
                set_decay(l, 0)
                for c in range(HEADS):
                    for s in range(steps_of(c)):
                        (hgrn if c < HG_HEADS else attend)(l, c, s)
                        if s == STACK_STEP and HG_HEADS <= c + 1 < HEADS:
                            stack_high(l, c + 1)
                        if s == mix_step(c) and c > 0:
                            round_mixed(l, c - 1)
                        if s == DECAY_STEP and c + 1 < HG_HEADS:
                            set_decay(l, c + 1)
                        for i in [*(units_left(c - 1) if s == 0 else ()), *units_after(c, s)]:
                            evacuate(l, i)
                round_mixed(l, HEADS - 1)
                for i in range(OUT_B, LAYER_UNITS):
                    evacuate(l, i)
                    square_h(l + 1, i - OUT_B)
            cut_u(DEPTH)

        @block.vector
        def _(dve):
            own = [0]

            def step(ins):
                own[0] += 1
                ins.then_inc(dve_step, 1)
                return own[0]

            def after(w):
                dve.wait_ge(dve_step, w)

            def prepare_lower_bounds():
                dve.wait_ge(consts_in, 16 * 8)
                w = step(dve.tensor_tensor(lb_work[:, 2, :], lb[:, 0, :], lb[:, 1, :], ALU.max))
                after(w)
                step(dve.tensor_tensor(lb_work[:, 0, :], lb[:, 0, :], lb_work[:, 2, :], ALU.subtract))
                dve.tensor_tensor(lb_work[:, 1, :], lb[:, 1, :], lb_work[:, 2, :], ALU.subtract)\
                    .then_inc(lb_max, 1)
                w = step(dve.tensor_tensor(lam_prod[:, :, :], lam_in[:, :, 0, :], lam_in[:, :, 1, :],
                                           ALU.mult))
                after(w)
                dve.tensor_reduce(lam_sum[:, :, :].rearrange("p a b -> p (a b)"), lam_prod[:, :, :],
                                  axis=X, op=ALU.add).then_inc(lb_max, 1)
                dve.wait_ge(lb_exp, 1)
                w = step(dve.tensor_tensor(lb_work[:, 2, :], lb_work[:, 0, :], lb_work[:, 1, :], ALU.add))
                after(w)
                w = step(dve.reciprocal(lb_work[:, 3, :], lb_work[:, 2, :]))
                after(w)
                step(dve.tensor_tensor(lb_work[:, 0, :], lb_work[:, 0, :], lb_work[:, 3, :], ALU.mult))
                w = step(dve.tensor_tensor(lb_work[:, 1, :], lb_work[:, 1, :], lb_work[:, 3, :], ALU.mult))
                after(w)
                w = step(dve.tensor_tensor(lb_work[:, 2, :], lb_work[:, 0, :], lb_work[:, 1, :], ALU.add))
                after(w)
                step(dve.tensor_tensor(lb[:, 0, :], lb_work[:, 0, :], lb_work[:, 0, :], ALU.subtract))
                w = step(dve.tensor_tensor(lb[:, 1, :], lb_work[:, 2, :], lb_work[:, 0, :], ALU.subtract))
                after(w)
                dve.tensor_scalar(one_minus_lb[:, :, :], lb[:, :, :], -1.0, 1.0, ALU.mult, ALU.add)\
                    .then_inc(bounds_ready, 1)
                dve.wait_ge(bounds_ready, 1)
                dve.wait_ge(lb_exp, 2)
                for l in range(DEPTH):
                    init = 0.8 - 0.6 * math.exp(-0.3 * l)
                    w = step(dve.tensor_tensor(lam[:, l:l + 1], lam_sum[:, l, 0:1], lam_sum[:, l, 1:2],
                                               ALU.subtract))
                    after(w)
                    step(dve.tensor_scalar(lam[:, l:l + 1], lam[:, l:l + 1], -1.0, -init, ALU.mult, ALU.add))
                    step(dve.tensor_scalar(g_at[:, l:l + 1], g_at[:, l:l + 1],
                                           math.sqrt(P) * (1.0 - init) * 0.5, None, ALU.mult))
                step(dve.tensor_scalar(g_hg[:, :], g_hg[:, :], math.sqrt(P), None, ALU.mult))
                w = step(dve.tensor_scalar(g_final[:, :], g_final[:, :], math.sqrt(D_MODEL), None, ALU.mult))
                after(w)

            def inverse_rms(roots):
                dve.wait_ge(root_ready, roots)
                return step(dve.reciprocal(sq[:, :], sq[:, :]))

            def norm_u(l):
                after(inverse_rms(l + 1))
                for k in range(KT + 1):
                    if k < KT:
                        if k >= 4:
                            dve.wait_ge(u_lo_ready, l * KT + k - 4 + 1)
                        dve.scalar_tensor_tensor(qk_dec[:, (k % 4) // 2, k % 2, :], h[:, k, :],
                                                 g_in[:, l, k:k + 1], sq[:, :], ALU.mult, ALU.mult)\
                            .then_inc(u_ready, 1)
                    if k > 0:
                        j = k - 1
                        dve.wait_ge(u_hi_ready, l * KT + j + 1)
                        dve.tensor_tensor(u_lo[:, j, :], qk_dec[:, (j % 4) // 2, j % 2, :],
                                          u_hi[:, j, :].bitcast(f32), ALU.subtract)\
                            .then_inc(u_lo_ready, 1)

            def norm_out():
                after(inverse_rms(DEPTH + 1))
                for k in range(KT):
                    dve.scalar_tensor_tensor(u_out(k), h[:, k, N_META:T], g_final[:, k:k + 1],
                                             sq[:, N_META:T], ALU.mult, ALU.mult).then_inc(out_ready, 1)

            def follow(l, i):
                what, c, j, _ = UNITS[i]
                t = l * LAYER_UNITS + i
                n = l * HEADS + c
                if what in ("outA", "outB"):
                    dve.wait_ge(unit_done, t + 1)
                    dve.tensor_tensor(two(h[:, j, :]), two(h[:, j, :]), proj[t % 2][:, :, both], ALU.add)\
                        .then_inc(evacuated[t % 2], 1)
                    return
                if what in ("q", "v", "av"):
                    return
                use = n * 3 + STAGE_USE[what]
                dve.wait_ge(evacuated[t % 2], evac_count(t))
                if use:
                    dve.wait_ge(stage_read, use)
                a, b = stage[:, use % 2, 0, :], stage[:, use % 2, 1, :]
                if what in ("zf", "zb"):
                    d = 0 if what == "zf" else 1
                    row = d * HG_HEADS + c
                    oml = one_minus_lb[:, l, row:row + 1]
                    w = step(dve.tensor_scalar(a, a, oml, lb[:, l, row:row + 1], ALU.mult, ALU.add))
                    after(w)
                    dve.tensor_scalar(gate_f[:, d, :], a, F_FLOOR, None, ALU.max)\
                        .then_inc(stage_read, 1)
                elif what == "g":
                    dve.tensor_tensor(gates[:, c % 2, :], a, b, ALU.mult).then_inc(stage_read, 1)
                elif what == "ag":
                    dve.scalar_tensor_tensor(gates[:, c % 2, :], a, 1.0, b, ALU.add, ALU.mult)\
                        .then_inc(stage_read, 1)
                else:
                    d = 0 if what == "aq" else 1
                    w = step(dve.stream_shuffle(b, a, [r ^ 1 for r in range(32)]))
                    after(w)
                    step(dve.tensor_tensor(a, a, cos_sin[:, 0, :], ALU.mult))
                    w = step(dve.tensor_tensor(b, b, cos_sin[:, 1, :], ALU.mult))
                    after(w)
                    if c > HG_HEADS:
                        dve.wait_ge(stack_lo, 4 * (l * AT_HEADS + c - HG_HEADS))
                    dve.tensor_tensor(gate_f[:, d, :], a, b, ALU.add).then_inc(stage_read, 1)

            def stack_low(a):
                for i, stack in enumerate((q_stack, k_stack)):
                    for comp, rows in enumerate(comps):
                        dve.wait_ge(stack_hi, 4 * a + 2 * i + comp + 1)
                        low = gate_f[rows, 2, :] if i == 0 else k_low[rows, :]
                        dve.tensor_tensor(low, gate_f[rows, i, :], stack[rows, comp, :].bitcast(f32),
                                           ALU.subtract).then_inc(stack_lo, 1)

            def copy_level(g, lv):
                dve.wait_ge(level_done, g * LEVELS + lv + 1)
                src = pair[:, lv % 2, :].rearrange("p (c n) -> p c n", c=N_CHUNKS)
                dve.wait_ge(level_read, g * LEVELS + lv)
                mask = masks[:, lv - 1, :].unsqueeze(1).to_broadcast([P, N_CHUNKS, P])
                dve.copy_predicated(score[:, :, :], mask, src).then_inc(level_read, 1)

            def copy_meta_levels(g):
                dve.wait_ge(level_done, g * LEVELS + META_LEVELS)
                w = step(dve.tensor_copy(score_meta[:, :], meta[0:N_META, 0:N_META]))
                for lv in range(1, META_LEVELS):
                    after(w)
                    ins = dve.copy_predicated(score_meta[:, :], masks[0:N_META, lv - 1, 0:N_META],
                                              meta[0:N_META, lv * N_META:(lv + 1) * N_META])
                    if lv < META_LEVELS - 1:
                        w = step(ins)
                    else:
                        ins.then_inc(meta_read, 1)

            last_decay = {}

            def level_products(g, c, lv):
                m = 2 ** (lv - 1)
                qkk_c, dst = qkk[:, c % 2, :, :], qk_dec[:, lv % 2, :, :]
                if lv == 1:
                    if c > 0:
                        dve.wait_ge(o_done, g)
                    dve.wait_ge(decay_set, 4 * (g + 1))
                if lv >= 2:
                    dve.wait_ge(level_done, g * LEVELS + lv - 1)
                    after(last_decay["second"])
                step(dve.tensor_tensor(block_half(dst, m, 1), block_half(qkk_c[:, 0:3:2, :], m, 1),
                                       block_half(decay[:, 0:2, :], m, 1), ALU.mult))
                if lv >= 2:
                    after(last_decay["first"])
                dve.tensor_tensor(block_half(dst, m, 0), block_half(qkk_c[:, 0:2, :], m, 0),
                                  block_half(decay[:, 2:4, :], m, 0), ALU.mult).then_inc(qk_ready, 1)
                if lv >= 2:
                    after(last_decay["totals"])
                first = 0 if m < N_META else N_META
                n_pairs = (T - first) // (2 * m)
                out_at = TOTALS_AT[2 * m]
                last_decay["totals"] = step(dve.tensor_tensor(
                    totals[:, :, out_at:out_at + n_pairs],
                    block_totals(slice(0, 3), m, 0), block_totals(slice(0, 3), m, 1), ALU.mult))

                def spread(a, half):
                    t = block_totals(a, m, half)
                    return t.unsqueeze(3).to_broadcast([P, 2, n_pairs, m])

                second = block_half(decay[:, 0:2, :], m, 1)
                last_decay["second"] = step(dve.tensor_tensor(second, second, spread(slice(0, 2), 0), ALU.mult))
                firsts = block_half(decay[:, 2:4, :], m, 0)
                last_decay["first"] = step(dve.tensor_tensor(firsts, firsts, spread(slice(1, 3), 1), ALU.mult))

            def chain_back(g):
                dve.wait_ge(kv_done, 2 * g + 1)
                w = step(dve.tensor_copy(state_b[:, 3, :], pair[:, 0, 3 * P:4 * P]))
                at = TOTALS_AT[P]
                for j in (2, 1, 0):
                    after(w)
                    w = step(dve.scalar_tensor_tensor(state_b[:, j, :], state_b[:, j + 1, :],
                                                      totals[:, 1, at + j:at + j + 1],
                                                      pair[:, 0, j * P:(j + 1) * P], ALU.mult, ALU.add))

            def chain_forward(g):
                dve.wait_ge(kv_done, 2 * g + 2)
                w = step(dve.tensor_copy(state_f[:, 0, :], pair[:, 1, 0:P]))
                at = TOTALS_AT[P]
                for j in range(3):
                    after(w)
                    ins = dve.scalar_tensor_tensor(state_f[:, j + 1, :], state_f[:, j, :],
                                                   totals[:, 0, at + j:at + j + 1],
                                                   pair[:, 1, (j + 1) * P:(j + 2) * P], ALU.mult, ALU.add)
                    if j < 2:
                        w = step(ins)
                    else:
                        ins.then_inc(states_ready, 1)

            def scale_output(n):
                dve.wait_ge(o_inv_ready, n + 1)
                rows = o_rows[:, 0:N_CHUNKS, :]
                step(dve.tensor_tensor(rows, rows, o_inv[:, 0:N_CHUNKS].unsqueeze(2)
                                       .to_broadcast([P, N_CHUNKS, P]), ALU.mult))
                rows = o_rows[0:N_META, N_CHUNKS, :]
                dve.tensor_scalar(rows, rows, o_inv[0:N_META, N_CHUNKS:N_CHUNKS + 1], None, ALU.mult)\
                    .then_inc(o_scaled, 1)

            def gate_main(l, c):
                n = l * HEADS + c
                gain = g_hg[:, l:l + 1] if c < HG_HEADS else g_at[:, l:l + 1]
                dve.wait_ge(o_turned, 2 * n + 1)
                dve.wait_ge(stage_read, 3 * n + 3)
                if n > 0:
                    dve.wait_ge(mix_lo_ready, n)
                step(dve.scalar_tensor_tensor(mixed_t[:, N_META:T], main[:, :], gain,
                                              gates[:, c % 2, N_META:T], ALU.mult, ALU.mult))

            def gate_meta(l, c):
                gain = g_hg[:, l:l + 1] if c < HG_HEADS else g_at[:, l:l + 1]
                dve.wait_ge(o_turned, 2 * (l * HEADS + c) + 2)
                dve.scalar_tensor_tensor(mixed_t[:, 0:N_META], meta[:, 0:N_META], gain,
                                         gates[:, c % 2, 0:N_META], ALU.mult, ALU.mult).then_inc(mixed, 1)

            def hgrn(l, c, s):
                n, g = l * HEADS + c, l * HG_HEADS + c
                if s == 0:
                    dve.wait_ge(k_scaled, 2 * (g + 1))
                    dve.tensor_tensor(qk_dec[:, 0, 1, :], qkk[:, c % 2, 1, :], qkk[:, c % 2, 2, :],
                                      ALU.add).then_inc(qk_ready, 1)
                elif s < LEVELS:
                    level_products(g, c, s)
                    if s >= 3:
                        copy_level(g, s - 2)
                    if s - 2 == META_LEVELS - 1:
                        copy_meta_levels(g)
                elif s == LEVELS:
                    dve.wait_ge(level_done, g * LEVELS + 7)
                    after(last_decay["first"])
                    dve.tensor_tensor(qk_dec[:, 0, :, :], qkk[:, c % 2, 0:3:2, :], decay[:, 0:2, :],
                                      ALU.mult).then_inc(qk_ready, 1)
                    copy_level(g, LEVELS - 2)
                elif s == TURN_KEYS:
                    copy_level(g, LEVELS - 1)
                    dve.tensor_tensor(qk_dec[:, 1, :, :], qkk[:, c % 2, 0:2, :], decay[:, 2:4, :],
                                      ALU.mult).then_inc(qk_ready, 1)
                    if c > 0:
                        gate_main(l, c - 1)
                elif s == TURN_KEYS + 1:
                    chain_back(g)
                elif s == TURN_KEYS + 2:
                    chain_forward(g)
                    if c > 0:
                        gate_meta(l, c - 1)

            def row_max(a, i, comp):
                rows = P if i < 4 else N_META
                dve.wait_ge(s_done, a * 10 + 2 * i + comp + 1)
                dve.tensor_reduce(neg_max[0:rows, i % 2, comp:comp + 1], pair[0:rows, :, both],
                                  axis=mybir.AxisListType.XY, op=ALU.max, negate=True)\
                    .then_inc(max_ready, 1)

            def attend(l, c, s):
                a = l * AT_HEADS + c - HG_HEADS
                i, comp = s // 2, s % 2
                if i < 5:
                    row_max(a, i, comp)
                if s == 1:
                    scale_output(l * HEADS + c - 1)
                elif s == 2:
                    gate_main(l, c - 1)
                    gate_meta(l, c - 1)
                if comp == 0 and 1 <= i < 6:
                    j = i - 1
                    r = slice(0, P if j < 4 else N_META)
                    dve.wait_ge(exp_done, a * 10 + 2 * j + 2)
                    w = step(dve.reciprocal(row_inv[r, j % 2, :], row_sum[r, j % 2, :]))
                    after(w)
                    w = step(dve.scalar_tensor_tensor(row_inv[r, j % 2, 1:2], row_inv[r, j % 2, 1:2],
                                                      lam[r, l:l + 1], row_sum[r, j % 2, 0:1],
                                                      ALU.mult, ALU.mult))
                    if j >= 2:
                        dve.wait_ge(p_turned, a * 5 + j - 1)
                    after(w)
                    e0, e1 = decay[r, 2 * (j % 2), :], decay[r, 2 * (j % 2) + 1, :]
                    dve.scalar_tensor_tensor(qk_dec[r, j % 2, 0, :], e1, row_inv[r, j % 2, 1:2], e0,
                                             ALU.mult, ALU.add).then_inc(p_ready, 1)

            prepare = True
            for l in range(DEPTH):
                if prepare:
                    dve.wait_ge(x_in, 16 * (KT + 1))
                    w = step(dve.tensor_scalar(g_in[:, :, :], g_in[:, :, :], math.sqrt(D_MODEL), None,
                                               ALU.mult))
                    after(w)
                norm_u(l)
                if prepare:
                    prepare_lower_bounds()
                    prepare = False
                for i in range(len(HG_TILES)):
                    follow(l, i)
                for c in range(HEADS):
                    for s in range(steps_of(c)):
                        (hgrn if c < HG_HEADS else attend)(l, c, s)
                        if s == STACK_STEP + 1 and HG_HEADS <= c + 1 < HEADS:
                            stack_low(l * AT_HEADS + c + 1 - HG_HEADS)
                        for i in units_followed(c, s):
                            follow(l, i)
                scale_output(l * HEADS + HEADS - 1)
                gate_main(l, HEADS - 1)
                gate_meta(l, HEADS - 1)
                for i in range(OUT_B, LAYER_UNITS):
                    follow(l, i)
            norm_out()

        @block.tensor
        def _(pe):
            def piece(l, i, k):
                what, c, j, _ = UNITS[i]
                t = l * LAYER_UNITS + i
                if k == 0:
                    pe.wait_ge(lo_cut, t + 1)
                    if t >= 2:
                        pe.wait_ge(evacuated[t % 2], evac_count(t - 2))
                    if what == "outA":
                        pe.wait_ge(mix_lo_ready, l * HEADS + HG_HEADS)
                if i == OUT_B:
                    pe.wait_ge(mix_lo_ready, l * HEADS + HG_HEADS + k + 1)
                if i == 0:
                    pe.wait_ge(u_lo_ready, l * KT + k + 1)
                hi, lo = (mix_hi, mix_lo) if what in ("outA", "outB") else (u_hi, u_lo)
                wh, wl = w_hi[:, t % N_CUT, k, :], w_lo[:, t % N_CUT, k, :]
                for w, x, p in ((wh, hi, 0), (wh, lo, 1), (wl, hi, 2)):
                    for n, cols_n in enumerate(halves):
                        ins = pe.matmul(proj[t % 2][:, n, both], w, x[:, k, cols_n],
                                        start=(k == 0 and p == 0), stop=(k == KT - 1 and p == 2))
                if k == KT - 1:
                    ins.then_inc(unit_done, 1)

            def feed(l, c, s):
                first, _ = fed_units(c)
                in_unit = EARLY_K if c == HEADS - 1 else KT
                for q in range(pieces_by(c, s - 1), pieces_by(c, s)):
                    piece(l, first + q // in_unit, q % in_unit)

            def sum_squares(n, k):
                if n == 0 and k == 0:
                    pe.wait_ge(ones_set, 4)
                pe.wait_ge(h_sq, n * KT + k + 1)
                for b, cols_n in enumerate(halves):
                    ins = pe.matmul(pair[:, b, both], ones[:, :], decay[:, k % 4, cols_n],
                                    start=(k == 0), stop=(k == KT - 1))
                ins.then_inc(h_sq_summed, 1)

            def turn_v(l, c):
                if l == 0 and c == 0:
                    pe.wait_ge(consts_in, 16 * 8)
                t = l * LAYER_UNITS + FIRST_UNIT[c] + (3 if c < HG_HEADS else 2)
                pe.wait_ge(evacuated[t % 2], evac_count(t))
                if l * HEADS + c > 0:
                    pe.wait_ge(o_taken, l * HEADS + c)
                for j in range(N_CHUNKS):
                    pe.transpose(main[:, j * P:(j + 1) * P], v_t[:, chunk(j)], ident[:, :])
                pe.transpose(meta[0:N_META, 0:P], v_t[:, 0:N_META], ident[:, :]).then_inc(v_turned, 1)

            def level(g, c, lv):
                pe.wait_ge(qk_ready, g * 10 + lv + 1)
                if lv >= 2:
                    pe.wait_ge(level_read, g * LEVELS + lv - 1)
                q = qkk[:, c % 2, 0, :] if lv == 0 else qk_dec[:, lv % 2, 0, :]
                k = qk_dec[:, lv % 2, 1, :]
                if lv < META_LEVELS:
                    pe.matmul(meta[0:N_META, lv * N_META:(lv + 1) * N_META], k[:, 0:N_META],
                              q[:, 0:N_META], start=True, stop=True)
                for j in range(N_CHUNKS):
                    ins = pe.matmul(pair[:, lv % 2, j * P:(j + 1) * P], k[:, chunk(j)], q[:, chunk(j)],
                                    start=True, stop=True)
                ins.then_inc(level_done, 1)

            def turn_main(n):
                pe.wait_ge(o_scaled, n + 1)
                for j in range(N_CHUNKS):
                    ins = pe.transpose(main[:, j * P:(j + 1) * P], o_rows[:, j, :], ident[:, :])
                ins.then_inc(o_turned, 1)

            def turn_meta(n):
                pe.transpose(meta[:, 0:N_META], o_rows[0:N_META, N_CHUNKS, :], ident[0:N_META, 0:N_META])\
                    .then_inc(o_turned, 1)

            def hgrn(l, c, s):
                n, g = l * HEADS + c, l * HG_HEADS + c
                if 1 <= s <= LEVELS:
                    if s == 1 and n > 0:
                        pe.wait_ge(o_taken, n)
                        if c > 0:
                            pe.wait_ge(states_ready, g)
                    level(g, c, s - 1)
                    if s == LEVELS:
                        pe.wait_ge(meta_read, g + 1)
                        turn_v(l, c)
                elif s == TURN_KEYS:
                    pe.wait_ge(qk_ready, g * 10 + 9)
                    pe.wait_ge(level_read, g * LEVELS + 7)
                    for j in range(N_CHUNKS):
                        ins = pe.transpose(pair[:, 0, j * P:(j + 1) * P], qk_dec[:, 0, 1, chunk(j)],
                                           ident[:, :])
                    ins.then_inc(k_turned, 1)
                    pe.wait_ge(v_ready, n + 1)
                    if c > 0:
                        turn_main(n - 1)
                elif s == TURN_KEYS + 1:
                    pe.wait_ge(qk_ready, g * 10 + 10)
                    pe.wait_ge(level_read, g * LEVELS + 8)
                    for j in range(N_CHUNKS - 1):
                        pe.transpose(pair[:, 1, j * P:(j + 1) * P], qk_dec[:, 1, 1, chunk(j)], ident[:, :])
                    pe.transpose(meta[0:N_META, 0:P], qk_dec[:, 1, 1, 0:N_META], ident[:, :])\
                        .then_inc(k_turned, 1)
                    pe.wait_ge(k_ready, 2 * g + 1)
                    for j in range(N_CHUNKS):
                        ins = pe.matmul(pair[:, 0, j * P:(j + 1) * P], cols[:, j, :], v_main[:, j, :],
                                        start=True, stop=True)
                    ins.then_inc(kv_done, 1)
                elif s == TURN_KEYS + 2:
                    pe.wait_ge(k_ready, 2 * g + 2)
                    pe.matmul(pair[:, 1, 0:P], cols[0:N_META, 7, :], v_meta[:, :], start=True, stop=True)
                    for j in range(N_CHUNKS - 1):
                        ins = pe.matmul(pair[:, 1, (j + 1) * P:(j + 2) * P], cols[:, 4 + j, :],
                                        v_main[:, j, :], start=True, stop=True)
                    ins.then_inc(kv_done, 1)
                    if c > 0:
                        turn_meta(n - 1)
                elif s == HG_STEPS - 1:
                    pe.wait_ge(states_ready, g + 1)
                    if c > 0:
                        pe.wait_ge(mixed, n)
                    for j in range(N_CHUNKS):
                        out = main[:, j * P:(j + 1) * P]
                        pe.matmul(out, score[:, j, :], v_main[:, j, :], start=True, stop=False)
                        pe.matmul(out, qk_dec[:, 0, 0, chunk(j)], state_f[:, j, :], start=False,
                                  stop=(j == 3))
                        if j < 3:
                            pe.matmul(out, qk_dec[:, 1, 0, chunk(j)], state_b[:, j + 1, :],
                                      start=False, stop=True)
                    out = meta[0:N_META, 0:P]
                    pe.matmul(out, score_meta[:, :], v_meta[:, :], start=True, stop=False)
                    pe.matmul(out, qk_dec[:, 1, 0, 0:N_META], state_b[:, 0, :], start=False, stop=True)\
                        .then_inc(o_done, 1)

            def attend(l, c, s):
                n, a = l * HEADS + c, l * AT_HEADS + c - HG_HEADS
                i, comp = s // 2, s % 2
                if s == 0:
                    pe.wait_ge(stacked, 16 * 4 * (a + 1))
                    pe.wait_ge(stack_lo, 4 * (a + 1))
                    if c == HG_HEADS:
                        pe.wait_ge(states_ready, (l + 1) * HG_HEADS)
                if i < 5:
                    rows = P if i < 4 else N_META
                    cs = chunk(i) if i < 4 else slice(0, N_META)
                    part = comps[comp]
                    if s > 0:
                        pe.wait_ge(exp_done, a * 10 + s)
                    for b, keys in enumerate(halves):
                        pe.matmul(pair[0:rows, b, both], q_stack[:, comp, cs], k_stack[:, comp, keys],
                                  start=True, stop=False)
                        ins = pe.matmul(pair[0:rows, b, both], q_stack[part, comp, cs], k_low[part, keys],
                                        start=False, stop=True)
                    ins.then_inc(s_done, 1)
                if s == 1:
                    turn_v(l, c)
                if s == 2:
                    pe.wait_ge(v_ready, n + 1)
                    turn_main(n - 1)
                    turn_meta(n - 1)
                if comp == 0 and 2 <= i < 7:
                    j = i - 2
                    rows = P if j < 4 else N_META
                    pe.wait_ge(pt_ready, a * 5 + j + 1)
                    for kk in range(4):
                        pe.matmul(meta[0:rows, 0:P], cols[:, kk, 0:rows], v_main[:, kk, :],
                                  start=(kk == 0), stop=False)
                    pe.matmul(meta[0:rows, 0:P], cols[0:N_META, 4, 0:rows], v_meta[:, :],
                              start=False, stop=True).then_inc(pv_done, 1)
                if comp == 1 and 1 <= i < 6:
                    j = i - 1
                    rows = P if j < 4 else N_META
                    if j == 0:
                        pe.wait_ge(mixed, n)
                    else:
                        pe.wait_ge(pv_read, a * 4 + j)
                    pe.wait_ge(p_ready, a * 5 + j + 1)
                    p = qk_dec[0:rows, j % 2, 0, :]
                    for kk in range(4):
                        pe.transpose(main[:, kk * P:kk * P + rows], p[:, chunk(kk)], ident[0:rows, 0:rows])
                    pe.transpose(meta[0:N_META, 0:rows], p[:, 0:N_META], ident[0:rows, 0:rows])\
                        .then_inc(p_turned, 1)

            for k in range(KT):
                sum_squares(0, k)
            for l in range(DEPTH):
                for i in range(len(HG_TILES)):
                    for k in range(KT):
                        piece(l, i, k)
                for c in range(HEADS):
                    for s in range(steps_of(c)):
                        (hgrn if c < HG_HEADS else attend)(l, c, s)
                        feed(l, c, s)
                for k in range(EARLY_FED - EARLY_K, EARLY_K):
                    piece(l, OUT_B + 1, k)
                pe.wait_ge(o_taken, (l + 1) * HEADS)
                turn_main(l * HEADS + HEADS - 1)
                turn_meta(l * HEADS + HEADS - 1)
                for j in range(OUT_TILES):
                    for k in range(EARLY_K if j < 2 else 0, KT):
                        piece(l, OUT_B + j, k)
                    if j > 0:
                        sum_squares(l + 1, j - 1)
                sum_squares(l + 1, OUT_TILES - 1)


def packed_weights(w_in, w_out):
    units = np.empty((DEPTH * LAYER_UNITS, P, KT, P), w_in.dtype)
    turn = np.arange(P).reshape(2, 2, 32).transpose(0, 2, 1).reshape(P)
    group = {"q": 0, "zf": 1, "zb": 2, "v": 3, "g": 4, "aq": 5, "ak": 6, "av": 7, "ag": 8}
    for l in range(DEPTH):
        for i, (what, c, j, _) in enumerate(UNITS):
            if what in ("outA", "outB"):
                rows = slice(0, D_MODEL) if what == "outA" else slice(D_MODEL, 2 * D_MODEL)
                tile = w_out[l][rows, j * P:(j + 1) * P]
            else:
                at = group[what] * D_MODEL + (c % HG_HEADS) * P
                tile = w_in[l][:, at:at + P]
                if what in ("aq", "ak"):
                    tile = tile[:, turn]
            units[l * LAYER_UNITS + i] = tile.reshape(KT, P, P).transpose(1, 0, 2)
    return units


def constants():
    s, t = np.meshgrid(np.arange(P), np.arange(P), indexing="ij")
    level = np.zeros((P, P), np.int64)
    for lv in range(1, LEVELS):
        level[(s ^ t) >= 2 ** (lv - 1)] = lv
    masks = np.stack([(level == lv) for lv in range(1, LEVELS)], axis=1).astype(np.int32)
    inv = np.float32(ROPE_THETA) ** (-np.arange(0, AT_HEAD_DIM, 2, dtype=np.float32) / np.float32(AT_HEAD_DIM))
    ang = np.arange(T, dtype=np.float32)[None, :] * inv.astype(np.float32)[:, None]
    rope = np.empty((P, 2, T), np.float32)
    row = np.arange(P)
    pair = (row % AT_HEAD_DIM) // 2
    rope[:, 0] = np.cos(ang)[pair]
    rope[:, 1] = np.sin(ang)[pair] * np.where(row % 2 == 0, -1.0, 1.0)[:, None]
    return masks, np.eye(P, dtype=np.float32), rope


def kernel(x, meta_tokens, norm_g, w_in, hg_lb_logits, hg_norm_g, diff_lambda, diff_subln_g,
           w_out, final_norm_g):
    import concourse.bacc as bacc
    from concourse.bass_utils import run_bass_kernel_spmd

    x, meta_tokens, norm_g, w_in, w_out = (np.asarray(a) for a in (x, meta_tokens, norm_g, w_in, w_out))
    hg_lb_logits, hg_norm_g, diff_lambda, diff_subln_g, final_norm_g = (
        np.asarray(a) for a in (hg_lb_logits, hg_norm_g, diff_lambda, diff_subln_g, final_norm_g))
    tokens = np.concatenate([meta_tokens, x[0]], axis=0)
    masks, identity, rope = constants()
    arrays = {
        "x_t": tokens.T.reshape(KT, P, T).transpose(1, 0, 2),
        "w_units": packed_weights(w_in, w_out),
        "norm_g": norm_g.reshape(DEPTH, KT, P).transpose(2, 0, 1),
        "lb_logits": hg_lb_logits.reshape(DEPTH, 2 * HG_HEADS, P).transpose(2, 0, 1),
        "hg_gain": hg_norm_g.T,
        "lambdas": np.broadcast_to(diff_lambda.reshape(1, DEPTH * 2, 2, AT_HEAD_DIM),
                                   (P, DEPTH * 2, 2, AT_HEAD_DIM)),
        "at_gain": diff_subln_g.T,
        "final_g": final_norm_g.reshape(KT, P).T,
        "level_masks": masks,
        "identity": identity,
        "rope": rope,
    }
    arrays = {k: np.ascontiguousarray(v) for k, v in arrays.items()}
    nc = bacc.Bacc("TRN2", target_bir_lowering=False, num_devices=1)
    args = [nc.dram_tensor(k, v.shape, mybir.dt.from_np(v.dtype), kind="ExternalInput").ap()
            for k, v in arrays.items()]
    out = nc.dram_tensor("out_t", (KT, P, SEQ), mybir.dt.float32, kind="ExternalOutput").ap()
    encoder_trunk(nc, *args, out)
    r = run_bass_kernel_spmd(nc, [arrays], core_ids=[0])
    return r.results[0]["out_t"].reshape(D_MODEL, SEQ).T.reshape(1, SEQ, D_MODEL)
```

```python
import math
from contextlib import ExitStack

import concourse.bass as bass
import numpy as np
from concourse import mybir

P = 128
DEPTH = 2
D_MODEL = 1024
N_META = 16
SEQ = 512
T = N_META + SEQ
HALF = T // 2
HG_HEADS = 8
AT_HEADS = 8
AT_HEAD_DIM = 64
HEADS = HG_HEADS + AT_HEADS
KT = D_MODEL // P
IN_TILES = 9216 // P
OUT_TILES = D_MODEL // P
NORM_EPS = 1e-6
F_FLOOR = 1e-30
ROPE_THETA = 10000.0
N_CHUNKS = SEQ // P
LEVELS = 8
META_LEVELS = 5
HG_TILES = ("zf", "zb", "q", "v", "g")
AT_TILES = ("aq", "ak", "av", "ag")
STAGE_USE = {"zf": 0, "zb": 1, "g": 2, "aq": 0, "ak": 1, "ag": 2}

TOTALS_AT = {}
_at = 0
for _m in (2, 4, 8, 16, 32, 64, 128):
    TOTALS_AT[_m] = _at
    _at += T // _m
TOTALS = _at


EARLY_TILES = 4
EARLY_K = KT - 1


def layer_units():
    units = []
    for c in range(HEADS):
        units += [(what, c, i, c - 1) for i, what in enumerate(HG_TILES if c < HG_HEADS else AT_TILES)]
        if c == HG_HEADS + 1:
            units += [("outA", c, j, c - 1) for j in range(OUT_TILES)]
    units += [("outB", HEADS, j, HEADS - 1) for j in range(EARLY_TILES)]
    units += [("outB", HEADS, j, HEADS) for j in range(EARLY_TILES, EARLY_TILES + 2)]
    units += [("outC", HEADS, 0, HEADS)]
    return units + [("outB", HEADS, j, HEADS) for j in range(EARLY_TILES + 2, OUT_TILES)]


UNITS = layer_units()
LAYER_UNITS = len(UNITS)
FIRST_UNIT = {c: next(i for i, u in enumerate(UNITS) if u[1] == c and u[0] != "outA") for c in range(HEADS)}
OUT_A_END = max(i for i, u in enumerate(UNITS) if u[0] == "outA") + 1
OUT_B = UNITS.index(("outB", HEADS, 0, HEADS - 1))
OUT_LATE = OUT_B + EARLY_TILES
OUT_C = OUT_LATE + 2
TILE_ORDER = (EARLY_TILES, EARLY_TILES + 1, *range(EARLY_TILES), *range(EARLY_TILES + 2, OUT_TILES))

TURN_KEYS = LEVELS + 1
HG_STEPS = LEVELS + 5
AT_STEPS = 2 * 6 + 1
DECAY_STEP = TURN_KEYS + 1
HG_FEED = (2, 3, 3, 3, 3, 3, 4, 4, 3, 3, 3, 4, 2)
AT_FEED = (3, 3, 3, 2, 2, 3, 2, 3, 2, 3, 2, 2, 2)
LAST_FEED = (2, 2, 1, 1, 3, 3, 3, 3, 2, 3, 2, 2, 1)


STACK_AFTER = {FIRST_UNIT[c] + (12 if c == HG_HEADS + 1 else 6): c - HG_HEADS for c in range(HG_HEADS, HEADS)}


def steps_of(c):
    return HG_STEPS if c < HG_HEADS else AT_STEPS


def mix_step(c):
    return HG_STEPS - 2 if c < HG_HEADS else 3


def stack_step(c):
    return HG_STEPS - 2 if c < HG_HEADS else 2 * 5 - 1


def share_fed(c, s):
    shares = HG_FEED if c < HG_HEADS else AT_FEED if c < HEADS - 1 else LAST_FEED
    return sum(shares[:s + 1]) / sum(shares)


def fed_units(c):
    fed = [i for i, u in enumerate(UNITS) if u[3] == c]
    return fed[0], fed[-1] + 1


def pieces_per_unit(c):
    return EARLY_K if c == HEADS - 1 else KT


def pieces_by(c, s):
    if s < 0:
        return 0
    first, last = fed_units(c)
    pieces = (last - first) * pieces_per_unit(c)
    return round(share_fed(c, s) * pieces)


def units_after(c, s):
    first, _ = fed_units(c)
    n = pieces_per_unit(c)
    return range(first + pieces_by(c, s - 2) // n, first + pieces_by(c, s - 1) // n)


def unit_of(tile):
    return next(i for i, u in enumerate(UNITS) if u[0] == "outB" and u[2] == tile)


def units_left(c):
    return units_after(c, steps_of(c)) if c >= 0 else ()


def units_followed(c, s):
    if c == HG_HEADS - 1:
        first = fed_units(c)[0]
        units = {TURN_KEYS: [first], TURN_KEYS + 1: [first + 1, first + 2]}.get(s, [])
    elif not HG_HEADS < c < HEADS - 1:
        units = [*units_after(c, s)]
    elif s % 2 == 1:
        units = [*units_after(c, s - 2), *units_after(c, s - 1)]
    else:
        units = []
    if s == 1 and c > 0:
        units = [*units_not_followed(c - 1), *units]
    return units


def units_not_followed(c):
    end = steps_of(c)
    late = [i for t in (end - 2, end - 1) for i in units_after(c, t)] if HG_HEADS < c < HEADS - 1 else []
    return [*late, *units_left(c)]


def encoder_trunk(nc, x_t, w_units, norm_g, lb_logits, hg_gain, lambdas, at_gain, final_g,
                  level_masks, identity, rope, out_t):
    f32 = mybir.dt.float32
    f32r = mybir.dt.float32r
    i32 = mybir.dt.int32
    ALU = mybir.AluOpType
    ACT = mybir.ActivationFunctionType
    X = mybir.AxisListType.X

    N_RAW = 2
    N_CUT = 3

    ctx = ExitStack()
    with ctx:
        def sb(name, shape, dt=f32):
            return ctx.enter_context(nc.sbuf_tensor(name, shape, dt))

        def sem(name):
            return ctx.enter_context(nc.semaphore(name))

        h = sb("h", [P, KT, T])
        u_hi = sb("u_hi", [P, KT, T], f32r)
        u_lo = sb("u_lo", [P, KT, T], f32r)
        mix_hi = sb("mix_hi", [P, 8, T], f32r)
        mix_lo = sb("mix_lo", [P, 8, T], f32r)
        w_raw = sb("w_raw", [P, N_RAW, KT, P])
        w_hi = sb("w_hi", [P, N_CUT, KT, P], f32r)
        w_lo = sb("w_lo", [P, N_CUT, KT, P], f32r)
        masks = sb("masks", [P, LEVELS - 1, P], i32)
        ident = sb("ident", [P, P])
        ones = sb("ones", [P, P])
        cos_sin = sb("cos_sin", [P, 2, T])
        g_in = sb("g_in", [P, DEPTH, KT])
        g_final = sb("g_final", [P, KT])
        g_hg = sb("g_hg", [P, DEPTH])
        g_at = sb("g_at", [P, DEPTH])
        lb = sb("lb", [P, DEPTH, 2 * HG_HEADS])
        one_minus_lb = sb("one_minus_lb", [P, DEPTH, 2 * HG_HEADS])
        lb_work = sb("lb_work", [P, 4, 2 * HG_HEADS])
        lam_sum = sb("lam_sum", [P, DEPTH, 2])
        lam = sb("lam", [P, DEPTH])
        stage = sb("stage", [P, 2, 2, T])
        gate_f = sb("gate_f", [P, 3, T])
        totals = sb("totals", [P, 3, TOTALS])
        decay = sb("decay", [P, 4, T])
        qkk = sb("qkk", [P, 2, 3, T])
        qk_dec = sb("qk_dec", [P, 2, 2, T])
        q_stack = sb("q_stack", [P, 2, T], f32r)
        k_stack = sb("k_stack", [P, 2, T], f32r)
        k_low = sb("k_low", [P, T], f32r)
        gates = sb("gates", [P, 2, T])
        v_t = sb("v_t", [P, T])
        v_main = sb("v_main", [P, N_CHUNKS, P])
        v_meta = sb("v_meta", [N_META, P])
        cols = sb("cols", [P, 2 * N_CHUNKS, P])
        state_f = sb("state_f", [P, N_CHUNKS, P])
        state_b = sb("state_b", [P, N_CHUNKS, P])
        lam_in = state_f[:, :, :].rearrange("p a (b d) -> p a b d", b=2)
        lam_prod = state_b[:, 0:DEPTH, :].rearrange("p a (b d) -> p (a b) d", b=2)
        score = sb("score", [P, N_CHUNKS, P])
        score_meta = sb("score_meta", [N_META, N_META])
        o_rows = sb("o_rows", [P, N_CHUNKS + 1, P])
        o_sums = sb("o_sums", [P, N_CHUNKS + 1])
        o_inv = sb("o_inv", [P, N_CHUNKS + 1])
        minus_half = sb("minus_half", [P, N_CHUNKS + 1])
        mixed_t = sb("mixed_t", [P, T])
        sq = mixed_t
        eps_count = sb("eps_count", [P, 1])
        warm = sb("warm", [P, 1])
        neg_max = sb("neg_max", [P, 2, 2])
        row_sum = sb("row_sum", [P, 2, 2])
        row_inv = sb("row_inv", [P, 2, 2])

        proj = [ctx.enter_context(nc.psum_tensor(f"proj{i}", [P, 2, 512], f32)) for i in range(2)]
        pair = ctx.enter_context(nc.psum_tensor("pair", [P, 2, 512], f32))
        main = ctx.enter_context(nc.psum_tensor("main", [P, 512], f32))
        meta = ctx.enter_context(nc.psum_tensor("meta", [P, 512], f32))

        consts_in = sem("consts_in")
        x_in = [sem(f"x_in{k}") for k in range(KT)]
        gain_in = sem("gain_in")
        raw_in = [sem(f"raw_in{i}") for i in range(N_RAW)]
        out_stored = sem("out_stored")
        ones_set = sem("ones_set")
        hi_cut = sem("hi_cut")
        lo_cut = sem("lo_cut")
        unit_done = sem("unit_done")
        evacuated = [sem(f"evacuated{i}") for i in range(2)]
        stage_read = sem("stage_read")
        decay_set = sem("decay_set")
        qk_ready = sem("qk_ready")
        level_done = sem("level_done")
        level_read = sem("level_read")
        meta_read = sem("meta_read")
        v_turned = sem("v_turned")
        v_ready = sem("v_ready")
        k_turned = sem("k_turned")
        k_ready = sem("k_ready")
        kv_done = sem("kv_done")
        states_ready = sem("states_ready")
        o_done = sem("o_done")
        sq_ready = sem("sq_ready")
        o_taken = sem("o_taken")
        o_inv_ready = sem("o_inv_ready")
        o_scaled = sem("o_scaled")
        o_turned = sem("o_turned")
        pool_step = sem("pool_step")
        root_ready = sem("root_ready")
        mixed = sem("mixed")
        mix_hi_ready = sem("mix_hi_ready")
        mix_lo_ready = sem("mix_lo_ready")
        s_done = sem("s_done")
        max_ready = sem("max_ready")
        exp_done = sem("exp_done")
        p_ready = sem("p_ready")
        p_turned = sem("p_turned")
        pt_ready = sem("pt_ready")
        pv_done = sem("pv_done")
        pv_read = sem("pv_read")
        h_sq = sem("h_sq")
        h_sq_added = sem("h_sq_added")
        h_sq_summed = sem("h_sq_summed")
        u_ready = sem("u_ready")
        u_hi_ready = sem("u_hi_ready")
        u_lo_ready = sem("u_lo_ready")
        out_ready = sem("out_ready")
        bounds_ready = sem("bounds_ready")
        last_done = sem("last_done")
        last_added = sem("last_added")
        k_scaled = sem("k_scaled")
        stack_hi = sem("stack_hi")
        stack_lo = sem("stack_lo")
        stacked = sem("stacked")
        lb_exp = sem("lb_exp")
        lb_max = sem("lb_max")
        act_step = sem("act_step")
        dve_step = sem("dve_step")

        halves = (slice(0, HALF), slice(HALF, T))
        comps = (slice(0, AT_HEAD_DIM), slice(AT_HEAD_DIM, P))
        both = slice(0, HALF)

        def chunk(c):
            return slice(N_META + c * P, N_META + (c + 1) * P)

        def evac_count(t):
            return t // 2 + 1

        def last_out(l, j):
            return pair if j % 2 == 0 else proj[(l * LAYER_UNITS + OUT_C) % 2]

        def squares(j):
            return slice((j % N_CHUNKS) * P, (j % N_CHUNKS + 1) * P)

        def two(ap):
            return ap.rearrange("p (h n) -> p h n", h=2)

        def block_half(x, m, half):
            first = 0 if m < N_META else N_META
            return x[:, :, first:T].rearrange("p a (b h m) -> p a b h m", h=2, m=m)[:, :, :, half, :]

        def block_totals(a, m, half):
            n = (T if m <= N_META else SEQ) // m
            skip = 1 if m == N_META else 0
            src = gate_f[:, a, 0:T] if m == 1 else \
                totals[:, a, TOTALS_AT[m] + skip:TOTALS_AT[m] + n]
            return src.rearrange("p a (b h) -> p a b h", h=2)[:, :, :, half]

        def u_out(k):
            if k < 4:
                return decay[:, k, N_META:T]
            return qkk[:, (k - 4) // 2, (k - 4) % 2, N_META:T]

        block = ctx.enter_context(nc.Block())

        @block.sync
        def _(sp):
            def stack_other(a):
                sp.wait_ge(stack_hi, 4 * (a + 1))
                for comp, rows in enumerate(comps):
                    sp.dma_start(k_stack[comps[1 - comp], comp, :].bitcast(f32),
                                 k_stack[rows, comp, :].bitcast(f32)).then_inc(stacked, 16)
                sp.wait_ge(stack_lo, 4 * a + 2)
                for comp, rows in enumerate(comps):
                    sp.dma_start(q_stack[comps[1 - comp], comp, :].bitcast(f32), gate_f[rows, 2, :])\
                        .then_inc(stacked, 16)

            for k in range(KT):
                sp.dma_start(h[:, k, :], x_t[:, k, :]).then_inc(x_in[k], 16)
            sp.dma_start(g_in[:, :, :], norm_g).then_inc(gain_in, 16)
            for u in range(DEPTH * LAYER_UNITS):
                if u == N_RAW:
                    for dst, src in ((ident[:, :], identity), (lb[:, :, :], lb_logits), (g_hg[:, :], hg_gain),
                                     (g_at[:, :], at_gain), (g_final[:, :], final_g),
                                     (masks[:, :, :], level_masks), (cos_sin[:, :, :], rope),
                                     (lam_in[:, :, :, :], lambdas)):
                        sp.dma_start(dst, src).then_inc(consts_in, 16)
                if u >= N_RAW:
                    sp.wait_ge(lo_cut, u - N_RAW + 1)
                sp.dma_start(w_raw[:, u % N_RAW, :, :], w_units[u]).then_inc(raw_in[u % N_RAW], 16)
                if u % LAYER_UNITS in STACK_AFTER:
                    stack_other(u // LAYER_UNITS * AT_HEADS + STACK_AFTER[u % LAYER_UNITS])
            for k in range(KT):
                sp.wait_ge(out_ready, k + 1)
                sp.dma_start(out_t[k], u_out(k)).then_inc(out_stored, 16)
            sp.wait_ge(out_stored, 16 * KT)

        @block.gpsimd
        def _(pool):
            pool.memset(ones[:, :], 1.0).then_inc(ones_set, 1)
            pool.memset(eps_count[:, :], D_MODEL * NORM_EPS).then_inc(ones_set, 1)
            pool.memset(o_sums[:, :], 0.0).then_inc(ones_set, 1)
            pool.memset(minus_half[:, :], -0.5).then_inc(ones_set, 1)

            def cut_low(u):
                pool.wait_ge(hi_cut, u + 1)
                pool.tensor_tensor(w_lo[:, u % N_CUT, :, :], w_raw[:, u % N_RAW, :, :],
                                   w_hi[:, u % N_CUT, :, :].bitcast(f32), ALU.subtract)\
                    .then_inc(lo_cut, 1)

            def set_decay(l, c):
                g = l * HG_HEADS + c
                if g > 0:
                    pool.wait_ge(qk_ready, 10 * g)
                if c == 0:
                    pool.wait_ge(h_sq_summed, l + 1)
                pool.memset(decay[:, 1, :], 1.0).then_inc(decay_set, 1)
                pool.memset(decay[:, 3, :], 1.0).then_inc(decay_set, 1)

            def invert_rms(n):
                pool.wait_ge(sq_ready, n + 1)
                if n > 0:
                    pool.wait_ge(o_scaled, n)
                pool.tensor_scalar(o_inv[:, :], o_sums[:, :], P * NORM_EPS, None, ALU.add)\
                    .then_inc(pool_step, 1)
                pool.wait_ge(pool_step, n + 1)
                pool.tensor_tensor(o_inv[:, :], o_inv[:, :], minus_half[:, :], ALU.pow)\
                    .then_inc(o_inv_ready, 1)

            def cut_mixed(n):
                pool.wait_ge(mix_hi_ready, n + 1)
                pool.tensor_tensor(mix_lo[:, n % 8, :], mixed_t[:, :],
                                   mix_hi[:, n % 8, :].bitcast(f32), ALU.subtract)\
                    .then_inc(mix_lo_ready, 1)

            for u in range(N_CUT):
                cut_low(u)
            for l in range(DEPTH):
                base = l * LAYER_UNITS

                def follow(units):
                    for i in units:
                        if base + i + N_CUT < DEPTH * LAYER_UNITS:
                            cut_low(base + i + N_CUT)

                set_decay(l, 0)
                follow(range(len(HG_TILES)))
                for c in range(HEADS):
                    n = l * HEADS + c
                    for s in range(steps_of(c)):
                        if s == mix_step(c) and c > 0:
                            cut_mixed(n - 1)
                        if s == DECAY_STEP and c + 1 < HG_HEADS:
                            set_decay(l, c + 1)
                        follow(units_after(c, s))
                    invert_rms(n)
                    follow(units_left(c))
                cut_mixed(l * HEADS + HEADS - 1)
                follow(range(OUT_LATE, LAYER_UNITS))

        @block.scalar
        def _(act):
            own = [0]
            first_squares = [0]

            def step(ins):
                own[0] += 1
                ins.then_inc(act_step, 1)
                return own[0]

            def cut_high(u):
                act.wait_ge(raw_in[u % N_RAW], 16 * (u // N_RAW + 1))
                if u >= N_CUT:
                    act.wait_ge(unit_done, u - N_CUT + 1)
                act.activation(w_hi[:, u % N_CUT, :, :], w_raw[:, u % N_RAW, :, :], ACT.Copy)\
                    .then_inc(hi_cut, 1)

            def square_h(n, k):
                tile = k
                if n == 0:
                    act.wait_ge(x_in[k], 16)
                else:
                    l, tile = n - 1, TILE_ORDER[k]
                    if tile < EARLY_TILES - 1:
                        act.wait_ge(last_added, l * (EARLY_TILES - 1) + tile + 1)
                    else:
                        t = l * LAYER_UNITS + (OUT_C if tile == EARLY_TILES - 1 else unit_of(tile))
                        act.wait_ge(evacuated[t % 2], evac_count(t))
                if k >= 4:
                    act.wait_ge(h_sq_added, n * (KT - 2) + max(k - 4, 1))
                act.activation(decay[:, k % 4, :], h[:, tile, :], ACT.Square).then_inc(h_sq, 1)

            def root(n):
                act.wait_ge(h_sq_summed, n + 1)
                act.activation(two(sq[:, :]), pair[:, :, both], ACT.Sqrt, bias=eps_count[:, :])\
                    .then_inc(root_ready, 1)

            def load_root_table():
                step(act.activation(warm[:, :], eps_count[:, :], ACT.Sqrt))

            def set_decay(l, c):
                g = l * HG_HEADS + c
                act.wait_ge(stage_read, 3 * (l * HEADS + c) + 2)
                if g > 0:
                    act.wait_ge(qk_ready, 10 * g)
                act.activation(decay[:, 0:4:2, :], gate_f[:, 0:2, :], ACT.Copy).then_inc(decay_set, 1)
                act.activation(gate_f[:, 2, :], gate_f[:, 0, :], ACT.Copy).then_inc(decay_set, 1)

            def cut_u(l):
                for k in range(KT):
                    act.wait_ge(u_ready, l * KT + k + 1)
                    act.activation(u_hi[:, k, :], qk_dec[:, (k % 4) // 2, k % 2, :], ACT.Copy)\
                        .then_inc(u_hi_ready, 1)

            def evacuate(l, i):
                what, c, j, _ = UNITS[i]
                t = l * LAYER_UNITS + i
                src = proj[t % 2][:, :, both]
                act.wait_ge(unit_done, t + 1)
                if what not in ("outA", "outB", "outC"):
                    use = (l * HEADS + c) * 3 + STAGE_USE.get(what, 0)
                    if what in HG_TILES and l * HG_HEADS + c > 0:
                        act.wait_ge(k_scaled, 2 * (l * HG_HEADS + c))
                    if what not in ("q", "v", "av") and use >= 2:
                        act.wait_ge(stage_read, use - 1)
                    a, b = two(stage[:, use % 2, 0, :]), two(stage[:, use % 2, 1, :])
                    done = evacuated[t % 2]
                    if what in ("zf", "zb"):
                        d = 0 if what == "zf" else 1
                        row = d * HG_HEADS + c
                        if t == 0:
                            act.wait_ge(bounds_ready, 1)
                        step(act.activation(a, src, ACT.Sigmoid))
                        act.activation(b, src, ACT.Sigmoid, scale=-1.0).then_inc(done, 1)
                        act.wait_ge(done, evac_count(t))
                        act.activation(qkk[:, c % 2, 1 + d, :], stage[:, use % 2, 1, :], ACT.Copy,
                                       scale=one_minus_lb[:, l, row:row + 1]).then_inc(k_scaled, 1)
                    elif what == "q":
                        act.activation(two(qkk[:, c % 2, 0, :]), src, ACT.Copy).then_inc(done, 1)
                    elif what in ("v", "av"):
                        act.activation(two(v_t[:, :]), src, ACT.Copy).then_inc(done, 1)
                    elif what in ("g", "ag"):
                        if what == "g":
                            step(act.activation(a, src, ACT.Sigmoid))
                        else:
                            step(act.activation(a, src, ACT.Tanh, scale=0.5))
                        act.activation(b, src, ACT.Copy).then_inc(done, 1)
                    else:
                        act.activation(a, src, ACT.Copy,
                                       scale=AT_HEAD_DIM ** -0.5 if what == "aq" else 1.0)\
                            .then_inc(done, 1)
                if t + N_CUT < DEPTH * LAYER_UNITS:
                    cut_high(t + N_CUT)

            def copy_v(n):
                act.wait_ge(v_turned, n + 1)
                step(act.activation(v_main[:, :, :], main[:, :].rearrange("p (c n) -> p c n", c=4), ACT.Copy))
                act.activation(v_meta[:, :], meta[0:N_META, 0:P], ACT.Copy).then_inc(v_ready, 1)

            def scale_output(n):
                act.wait_ge(o_inv_ready, n + 1)
                for j in range(N_CHUNKS + 1):
                    rows = P if j < N_CHUNKS else N_META
                    ins = act.activation(o_rows[0:rows, j, :], o_rows[0:rows, j, :], ACT.Copy,
                                         scale=o_inv[0:rows, j:j + 1])
                    if j < N_CHUNKS:
                        step(ins)
                    else:
                        ins.then_inc(o_scaled, 1)

            def copy_diagonal(g):
                act.wait_ge(level_done, g * LEVELS + 1)
                act.activation(score[:, :, :], pair[:, 0, :].rearrange("p (c n) -> p c n", c=N_CHUNKS),
                               ACT.Copy).then_inc(level_read, 1)

            def hgrn(l, c, s):
                n, g = l * HEADS + c, l * HG_HEADS + c
                if s == 1:
                    copy_diagonal(g)
                if s == 2 and c > 0:
                    scale_output(n - 1)
                if s == TURN_KEYS:
                    copy_v(n)
                    act.wait_ge(k_turned, 2 * g + 1)
                    act.activation(cols[:, 0:4, :], pair[:, 0, :].rearrange("p (c n) -> p c n", c=4),
                                   ACT.Copy).then_inc(k_ready, 1)
                if s == TURN_KEYS + 1:
                    act.wait_ge(k_turned, 2 * g + 2)
                    step(act.activation(cols[:, 4:7, :],
                                        pair[:, 1, 0:3 * P].rearrange("p (c n) -> p c n", c=3), ACT.Copy))
                    act.activation(cols[0:N_META, 7, :], meta[0:N_META, 0:P], ACT.Copy)\
                        .then_inc(k_ready, 1)
                if s == HG_STEPS - 1:
                    if n > 0:
                        act.wait_ge(o_turned, 2 * n)
                    act.wait_ge(o_done, g + 1)
                    step(act.activation(o_rows[:, 0:N_CHUNKS, :],
                                        main[:, :].rearrange("p (c n) -> p c n", c=4), ACT.Copy))
                    act.activation(o_rows[0:N_META, N_CHUNKS, :], meta[0:N_META, 0:P], ACT.Copy)\
                        .then_inc(o_taken, 1)
                    act.wait_ge(o_taken, n + 1)
                    for j in range(N_CHUNKS + 1):
                        rows = P if j < N_CHUNKS else N_META
                        ins = act.activation(cols[0:rows, j, :], o_rows[0:rows, j, :], ACT.Square,
                                             accum_out=o_sums[0:rows, j:j + 1])
                        if j < N_CHUNKS:
                            step(ins)
                        else:
                            ins.then_inc(sq_ready, 1)

            def attend(l, c, s):
                n, a = l * HEADS + c, l * AT_HEADS + c - HG_HEADS
                i, comp = s // 2, s % 2
                if i < 5:
                    rows = P if i < 4 else N_META
                    if comp == 0 and i >= 2:
                        act.wait_ge(p_ready, a * 5 + i - 1)
                    act.wait_ge(max_ready, a * 10 + 2 * i + comp + 1)
                    act.activation(two(decay[0:rows, 2 * (i % 2) + comp, :]), pair[0:rows, :, both],
                                   ACT.Exp, bias=neg_max[0:rows, i % 2, comp:comp + 1],
                                   accum_out=row_sum[0:rows, i % 2, comp:comp + 1]).then_inc(exp_done, 1)
                if s == 1:
                    copy_v(n)
                if comp == 0 and 2 <= i < 7:
                    j = i - 2
                    rows = P if j < 4 else N_META
                    if j == 0:
                        act.wait_ge(o_turned, 2 * n)
                        act.wait_ge(mix_lo_ready, n)
                    act.wait_ge(pv_done, a * 5 + j + 1)
                    inv = row_inv[0:rows, j % 2, 0:1]
                    act.activation(o_rows[0:rows, j, :], meta[0:rows, 0:P], ACT.Copy, scale=inv)\
                        .then_inc(pv_read if j < 4 else o_taken, 1)
                    if j < 4:
                        act.wait_ge(pv_read, a * 4 + j + 1)
                    else:
                        act.wait_ge(o_taken, n + 1)
                        act.wait_ge(act_step, first_squares[0])
                    act.activation(sq[0:rows, squares(j)], o_rows[0:rows, j, :], ACT.Square,
                                   accum_out=o_sums[0:rows, j:j + 1]).then_inc(act_step if j < 4 else sq_ready, 1)
                    if j < 4:
                        own[0] += 1
                    if j == 0:
                        first_squares[0] = own[0]
                if comp == 1 and 1 <= i < 6:
                    j = i - 1
                    rows = P if j < 4 else N_META
                    act.wait_ge(p_turned, a * 5 + j + 1)
                    step(act.activation(cols[:, 0:4, 0:rows],
                                        main[:, :].rearrange("p (c n) -> p c n", c=4)[:, :, 0:rows],
                                        ACT.Copy))
                    act.activation(cols[0:N_META, 4, 0:rows], meta[0:N_META, 0:rows], ACT.Copy)\
                        .then_inc(pt_ready, 1)

            def stack_high(l, c):
                a = l * AT_HEADS + c - HG_HEADS
                act.wait_ge(stage_read, 3 * (l * HEADS + c) + 2)
                for i, stack in enumerate((q_stack, k_stack)):
                    for comp, rows in enumerate(comps):
                        act.activation(stack[rows, comp, :], gate_f[rows, i, :], ACT.Copy)\
                            .then_inc(stack_hi, 1)

            def round_mixed(l, c):
                n = l * HEADS + c
                if c >= HG_HEADS:
                    act.wait_ge(unit_done, l * LAYER_UNITS + OUT_A_END)
                act.wait_ge(mixed, n + 1)
                act.activation(mix_hi[:, c % 8, :], mixed_t[:, :], ACT.Copy).then_inc(mix_hi_ready, 1)

            act.wait_ge(ones_set, 4)
            load_root_table()
            for k in range(KT):
                square_h(0, k)
            cut_high(0)
            root(0)
            for u in range(1, N_CUT):
                cut_high(u)
            for l in range(DEPTH):
                cut_u(l)
                if l == 0:
                    act.wait_ge(lb_max, 1)
                    act.activation(lb_work[:, 0:2, :], lb_work[:, 0:2, :], ACT.Exp).then_inc(lb_exp, 1)
                    act.wait_ge(lb_max, 2)
                    act.activation(lam_sum[:, :, :], lam_sum[:, :, :], ACT.Exp).then_inc(lb_exp, 1)
                for i in range(len(HG_TILES)):
                    evacuate(l, i)
                    if i == 2:
                        set_decay(l, 0)
                for c in range(HEADS):
                    for s in range(steps_of(c)):
                        (hgrn if c < HG_HEADS else attend)(l, c, s)
                        if s == stack_step(c) and HG_HEADS <= c + 1 < HEADS:
                            stack_high(l, c + 1)
                        if s == mix_step(c) and c > 0:
                            round_mixed(l, c - 1)
                        if s == DECAY_STEP and c + 1 < HG_HEADS:
                            set_decay(l, c + 1)
                        for i in [*(units_left(c - 1) if s == 0 else ()), *units_after(c, s)]:
                            evacuate(l, i)
                for i in units_left(HEADS - 1):
                    evacuate(l, i)
                round_mixed(l, HEADS - 1)
                act.wait_ge(act_step, own[0])
                load_root_table()
                k = 0
                for i in range(OUT_LATE, LAYER_UNITS):
                    if i < OUT_C:
                        evacuate(l, i)
                    for _ in range(EARLY_TILES if i == OUT_C else 1):
                        square_h(l + 1, k)
                        k += 1
                    if i >= OUT_C:
                        evacuate(l, i)
                root(l + 1)

        @block.vector
        def _(dve):
            own = [0]

            def step(ins):
                own[0] += 1
                ins.then_inc(dve_step, 1)
                return own[0]

            def after(w):
                dve.wait_ge(dve_step, w)

            def prepare_lower_bounds():
                dve.wait_ge(consts_in, 16 * 8)
                w = step(dve.tensor_tensor(lb_work[:, 2, :], lb[:, 0, :], lb[:, 1, :], ALU.max))
                after(w)
                step(dve.tensor_tensor(lb_work[:, 0, :], lb[:, 0, :], lb_work[:, 2, :], ALU.subtract))
                dve.tensor_tensor(lb_work[:, 1, :], lb[:, 1, :], lb_work[:, 2, :], ALU.subtract)\
                    .then_inc(lb_max, 1)
                w = step(dve.tensor_tensor(lam_prod[:, :, :], lam_in[:, :, 0, :], lam_in[:, :, 1, :],
                                           ALU.mult))
                after(w)
                dve.tensor_reduce(lam_sum[:, :, :].rearrange("p a b -> p (a b)"), lam_prod[:, :, :],
                                  axis=X, op=ALU.add).then_inc(lb_max, 1)
                dve.wait_ge(lb_exp, 1)
                w = step(dve.tensor_tensor(lb_work[:, 2, :], lb_work[:, 0, :], lb_work[:, 1, :], ALU.add))
                after(w)
                w = step(dve.reciprocal(lb_work[:, 3, :], lb_work[:, 2, :]))
                after(w)
                step(dve.tensor_tensor(lb_work[:, 0, :], lb_work[:, 0, :], lb_work[:, 3, :], ALU.mult))
                w = step(dve.tensor_tensor(lb_work[:, 1, :], lb_work[:, 1, :], lb_work[:, 3, :], ALU.mult))
                after(w)
                w = step(dve.tensor_tensor(lb_work[:, 2, :], lb_work[:, 0, :], lb_work[:, 1, :], ALU.add))
                after(w)
                step(dve.tensor_tensor(lb[:, 0, :], lb_work[:, 0, :], lb_work[:, 0, :], ALU.subtract))
                w = step(dve.tensor_tensor(lb[:, 1, :], lb_work[:, 2, :], lb_work[:, 0, :], ALU.subtract))
                after(w)
                dve.tensor_scalar(one_minus_lb[:, :, :], lb[:, :, :], -1.0, 1.0, ALU.mult, ALU.add)\
                    .then_inc(bounds_ready, 1)
                dve.wait_ge(bounds_ready, 1)
                dve.wait_ge(lb_exp, 2)
                for l in range(DEPTH):
                    init = 0.8 - 0.6 * math.exp(-0.3 * l)
                    w = step(dve.tensor_tensor(lam[:, l:l + 1], lam_sum[:, l, 0:1], lam_sum[:, l, 1:2],
                                               ALU.subtract))
                    after(w)
                    step(dve.tensor_scalar(lam[:, l:l + 1], lam[:, l:l + 1], -1.0, -init, ALU.mult, ALU.add))
                    step(dve.tensor_scalar(g_at[:, l:l + 1], g_at[:, l:l + 1],
                                           math.sqrt(P) * (1.0 - init) * 0.5, None, ALU.mult))
                step(dve.tensor_scalar(g_hg[:, :], g_hg[:, :], math.sqrt(P), None, ALU.mult))
                w = step(dve.tensor_scalar(g_final[:, :], g_final[:, :], math.sqrt(D_MODEL), None, ALU.mult))
                after(w)

            def add_squares(n, k):
                dve.wait_ge(h_sq, n * KT + k + 1)
                if k > 1:
                    dve.wait_ge(h_sq_added, n * (KT - 2) + k - 1)
                dve.tensor_tensor(sq[:, :], decay[:, 0, :] if k == 1 else sq[:, :], decay[:, k % 4, :],
                                  ALU.add).then_inc(h_sq_added, 1)

            def invert_roots(n):
                dve.wait_ge(root_ready, n + 1)
                after(step(dve.reciprocal(sq[:, :], sq[:, :])))

            def norm_u(l):
                invert_roots(l)
                for k in range(KT + 1):
                    if k < KT:
                        if k >= 4:
                            dve.wait_ge(u_lo_ready, l * KT + k - 4 + 1)
                        dve.scalar_tensor_tensor(qk_dec[:, (k % 4) // 2, k % 2, :], h[:, k, :],
                                                 g_in[:, l, k:k + 1], sq[:, :], ALU.mult, ALU.mult)\
                            .then_inc(u_ready, 1)
                    if k > 0:
                        j = k - 1
                        dve.wait_ge(u_hi_ready, l * KT + j + 1)
                        dve.tensor_tensor(u_lo[:, j, :], qk_dec[:, (j % 4) // 2, j % 2, :],
                                          u_hi[:, j, :].bitcast(f32), ALU.subtract)\
                            .then_inc(u_lo_ready, 1)

            def norm_out():
                invert_roots(DEPTH)
                for k in range(KT):
                    dve.scalar_tensor_tensor(u_out(k), h[:, k, N_META:T], g_final[:, k:k + 1],
                                             sq[:, N_META:T], ALU.mult, ALU.mult).then_inc(out_ready, 1)

            def follow(l, i):
                what, c, j, _ = UNITS[i]
                t = l * LAYER_UNITS + i
                n = l * HEADS + c
                if what in ("outA", "outB"):
                    dve.wait_ge(unit_done, t + 1)
                    dve.tensor_tensor(two(h[:, j, :]), two(h[:, j, :]), proj[t % 2][:, :, both], ALU.add)\
                        .then_inc(evacuated[t % 2], 1)
                    return
                if what in ("q", "v", "av"):
                    return
                if what == "outC":
                    for tile in range(EARLY_TILES):
                        first = l * LAYER_UNITS + unit_of(tile)
                        dve.wait_ge(evacuated[first % 2], evac_count(first))
                        if tile < EARLY_TILES - 1:
                            dve.wait_ge(last_done, l * (EARLY_TILES - 1) + tile + 1)
                        else:
                            dve.wait_ge(unit_done, t + 1)
                        dve.tensor_tensor(two(h[:, tile, :]), two(h[:, tile, :]),
                                          last_out(l, tile)[:, :, both], ALU.add)\
                            .then_inc(last_added if tile < EARLY_TILES - 1 else evacuated[t % 2], 1)
                        add_squares(l + 1, TILE_ORDER.index(tile) - 1)
                    return
                use = n * 3 + STAGE_USE[what]
                dve.wait_ge(evacuated[t % 2], evac_count(t))
                if use:
                    dve.wait_ge(stage_read, use)
                a, b = stage[:, use % 2, 0, :], stage[:, use % 2, 1, :]
                if what in ("zf", "zb"):
                    d = 0 if what == "zf" else 1
                    row = d * HG_HEADS + c
                    oml = one_minus_lb[:, l, row:row + 1]
                    w = step(dve.tensor_scalar(a, a, oml, lb[:, l, row:row + 1], ALU.mult, ALU.add))
                    after(w)
                    dve.tensor_scalar(gate_f[:, d, :], a, F_FLOOR, None, ALU.max)\
                        .then_inc(stage_read, 1)
                elif what == "g":
                    dve.tensor_tensor(gates[:, c % 2, :], a, b, ALU.mult).then_inc(stage_read, 1)
                elif what == "ag":
                    dve.scalar_tensor_tensor(gates[:, c % 2, :], a, 1.0, b, ALU.add, ALU.mult)\
                        .then_inc(stage_read, 1)
                else:
                    d = 0 if what == "aq" else 1
                    w = step(dve.stream_shuffle(b, a, [r ^ 1 for r in range(32)]))
                    after(w)
                    step(dve.tensor_tensor(a, a, cos_sin[:, 0, :], ALU.mult))
                    w = step(dve.tensor_tensor(b, b, cos_sin[:, 1, :], ALU.mult))
                    after(w)
                    if c > HG_HEADS:
                        dve.wait_ge(stack_lo, 4 * (l * AT_HEADS + c - HG_HEADS))
                    dve.tensor_tensor(gate_f[:, d, :], a, b, ALU.add).then_inc(stage_read, 1)

            def stack_low(a):
                for i, stack in enumerate((q_stack, k_stack)):
                    for comp, rows in enumerate(comps):
                        dve.wait_ge(stack_hi, 4 * a + 2 * i + comp + 1)
                        low = gate_f[rows, 2, :] if i == 0 else k_low[rows, :]
                        dve.tensor_tensor(low, gate_f[rows, i, :], stack[rows, comp, :].bitcast(f32),
                                           ALU.subtract).then_inc(stack_lo, 1)

            def copy_level(g, lv):
                dve.wait_ge(level_done, g * LEVELS + lv + 1)
                src = pair[:, lv % 2, :].rearrange("p (c n) -> p c n", c=N_CHUNKS)
                dve.wait_ge(level_read, g * LEVELS + lv)
                mask = masks[:, lv - 1, :].unsqueeze(1).to_broadcast([P, N_CHUNKS, P])
                dve.copy_predicated(score[:, :, :], mask, src).then_inc(level_read, 1)

            def copy_meta_levels(g):
                dve.wait_ge(level_done, g * LEVELS + META_LEVELS)
                w = step(dve.tensor_copy(score_meta[:, :], meta[0:N_META, 0:N_META]))
                for lv in range(1, META_LEVELS):
                    after(w)
                    ins = dve.copy_predicated(score_meta[:, :], masks[0:N_META, lv - 1, 0:N_META],
                                              meta[0:N_META, lv * N_META:(lv + 1) * N_META])
                    if lv < META_LEVELS - 1:
                        w = step(ins)
                    else:
                        ins.then_inc(meta_read, 1)

            last_decay = {}

            def level_products(g, c, lv, copied=None):
                m = 2 ** (lv - 1)
                qkk_c, dst = qkk[:, c % 2, :, :], qk_dec[:, lv % 2, :, :]
                if lv == 1:
                    if c > 0:
                        dve.wait_ge(o_done, g)
                    dve.wait_ge(decay_set, 4 * (g + 1))
                if lv >= 2:
                    dve.wait_ge(level_done, g * LEVELS + lv - 1)
                    after(last_decay["second"])
                step(dve.tensor_tensor(block_half(dst, m, 1), block_half(qkk_c[:, 0:3:2, :], m, 1),
                                       block_half(decay[:, 0:2, :], m, 1), ALU.mult))
                if lv >= 2:
                    after(last_decay["first"])
                dve.tensor_tensor(block_half(dst, m, 0), block_half(qkk_c[:, 0:2, :], m, 0),
                                  block_half(decay[:, 2:4, :], m, 0), ALU.mult).then_inc(qk_ready, 1)
                if copied is not None:
                    copy_level(g, copied)
                if lv >= 2:
                    after(last_decay["totals"])
                first = 0 if m < N_META else N_META
                n_pairs = (T - first) // (2 * m)
                out_at = TOTALS_AT[2 * m]
                last_decay["totals"] = step(dve.tensor_tensor(
                    totals[:, :, out_at:out_at + n_pairs],
                    block_totals(slice(0, 3), m, 0), block_totals(slice(0, 3), m, 1), ALU.mult))

                def spread(a, half):
                    t = block_totals(a, m, half)
                    return t.unsqueeze(3).to_broadcast([P, 2, n_pairs, m])

                second = block_half(decay[:, 0:2, :], m, 1)
                last_decay["second"] = step(dve.tensor_tensor(second, second, spread(slice(0, 2), 0), ALU.mult))
                firsts = block_half(decay[:, 2:4, :], m, 0)
                last_decay["first"] = step(dve.tensor_tensor(firsts, firsts, spread(slice(1, 3), 1), ALU.mult))

            def chain_back(g):
                dve.wait_ge(kv_done, 2 * g + 1)
                w = step(dve.tensor_copy(state_b[:, 3, :], pair[:, 0, 3 * P:4 * P]))
                at = TOTALS_AT[P]
                for j in (2, 1, 0):
                    after(w)
                    w = step(dve.scalar_tensor_tensor(state_b[:, j, :], state_b[:, j + 1, :],
                                                      totals[:, 1, at + j:at + j + 1],
                                                      pair[:, 0, j * P:(j + 1) * P], ALU.mult, ALU.add))

            def chain_forward(g):
                dve.wait_ge(kv_done, 2 * g + 2)
                w = step(dve.tensor_copy(state_f[:, 0, :], pair[:, 1, 0:P]))
                at = TOTALS_AT[P]
                for j in range(3):
                    after(w)
                    ins = dve.scalar_tensor_tensor(state_f[:, j + 1, :], state_f[:, j, :],
                                                   totals[:, 0, at + j:at + j + 1],
                                                   pair[:, 1, (j + 1) * P:(j + 2) * P], ALU.mult, ALU.add)
                    if j < 2:
                        w = step(ins)
                    else:
                        ins.then_inc(states_ready, 1)

            def scale_output(n):
                dve.wait_ge(o_inv_ready, n + 1)
                rows = o_rows[:, 0:N_CHUNKS, :]
                step(dve.tensor_tensor(rows, rows, o_inv[:, 0:N_CHUNKS].unsqueeze(2)
                                       .to_broadcast([P, N_CHUNKS, P]), ALU.mult))
                rows = o_rows[0:N_META, N_CHUNKS, :]
                dve.tensor_scalar(rows, rows, o_inv[0:N_META, N_CHUNKS:N_CHUNKS + 1], None, ALU.mult)\
                    .then_inc(o_scaled, 1)

            def gate_main(l, c):
                n = l * HEADS + c
                gain = g_hg[:, l:l + 1] if c < HG_HEADS else g_at[:, l:l + 1]
                dve.wait_ge(o_turned, 2 * n + 1)
                dve.wait_ge(stage_read, 3 * n + 3)
                if n > 0:
                    dve.wait_ge(mix_lo_ready, n)
                step(dve.scalar_tensor_tensor(mixed_t[:, N_META:T], main[:, :], gain,
                                              gates[:, c % 2, N_META:T], ALU.mult, ALU.mult))

            def gate_meta(l, c):
                gain = g_hg[:, l:l + 1] if c < HG_HEADS else g_at[:, l:l + 1]
                dve.wait_ge(o_turned, 2 * (l * HEADS + c) + 2)
                dve.scalar_tensor_tensor(mixed_t[:, 0:N_META], meta[:, 0:N_META], gain,
                                         gates[:, c % 2, 0:N_META], ALU.mult, ALU.mult).then_inc(mixed, 1)

            def hgrn(l, c, s):
                n, g = l * HEADS + c, l * HG_HEADS + c
                if s == 0:
                    dve.wait_ge(k_scaled, 2 * (g + 1))
                    dve.tensor_tensor(qk_dec[:, 0, 1, :], qkk[:, c % 2, 1, :], qkk[:, c % 2, 2, :],
                                      ALU.add).then_inc(qk_ready, 1)
                elif s < LEVELS:
                    level_products(g, c, s, copied=s - 2 if s >= META_LEVELS else None)
                    if 3 <= s < META_LEVELS:
                        copy_level(g, s - 2)
                    if s - 2 == META_LEVELS - 1:
                        copy_meta_levels(g)
                elif s == LEVELS:
                    dve.wait_ge(level_done, g * LEVELS + 7)
                    after(last_decay["first"])
                    dve.tensor_tensor(qk_dec[:, 0, :, :], qkk[:, c % 2, 0:3:2, :], decay[:, 0:2, :],
                                      ALU.mult).then_inc(qk_ready, 1)
                    copy_level(g, LEVELS - 2)
                elif s == TURN_KEYS:
                    copy_level(g, LEVELS - 1)
                    dve.tensor_tensor(qk_dec[:, 1, :, :], qkk[:, c % 2, 0:2, :], decay[:, 2:4, :],
                                      ALU.mult).then_inc(qk_ready, 1)
                    if c > 0:
                        gate_main(l, c - 1)
                elif s == TURN_KEYS + 1:
                    chain_back(g)
                elif s == TURN_KEYS + 2:
                    chain_forward(g)
                    if c > 0:
                        gate_meta(l, c - 1)

            def row_max(a, i, comp):
                rows = P if i < 4 else N_META
                dve.wait_ge(s_done, a * 10 + 2 * i + comp + 1)
                dve.tensor_reduce(neg_max[0:rows, i % 2, comp:comp + 1], pair[0:rows, :, both],
                                  axis=mybir.AxisListType.XY, op=ALU.max, negate=True)\
                    .then_inc(max_ready, 1)

            def attend(l, c, s):
                a = l * AT_HEADS + c - HG_HEADS
                i, comp = s // 2, s % 2
                if i < 5:
                    row_max(a, i, comp)
                if s == 1:
                    scale_output(l * HEADS + c - 1)
                elif s == 2:
                    gate_main(l, c - 1)
                    gate_meta(l, c - 1)
                if comp == 0 and 1 <= i < 6:
                    j = i - 1
                    r = slice(0, P if j < 4 else N_META)
                    dve.wait_ge(exp_done, a * 10 + 2 * j + 2)
                    w = step(dve.reciprocal(row_inv[r, j % 2, :], row_sum[r, j % 2, :]))
                    after(w)
                    w = step(dve.scalar_tensor_tensor(row_inv[r, j % 2, 1:2], row_inv[r, j % 2, 1:2],
                                                      lam[r, l:l + 1], row_sum[r, j % 2, 0:1],
                                                      ALU.mult, ALU.mult))
                    if j >= 2:
                        dve.wait_ge(p_turned, a * 5 + j - 1)
                    after(w)
                    e0, e1 = decay[r, 2 * (j % 2), :], decay[r, 2 * (j % 2) + 1, :]
                    dve.scalar_tensor_tensor(qk_dec[r, j % 2, 0, :], e1, row_inv[r, j % 2, 1:2], e0,
                                             ALU.mult, ALU.add).then_inc(p_ready, 1)

            for k in range(1, KT - 1):
                add_squares(0, k)
            dve.wait_ge(gain_in, 16)
            for k in range(KT):
                dve.wait_ge(x_in[k], 16)
            after(step(dve.tensor_scalar(g_in[:, :, :], g_in[:, :, :], math.sqrt(D_MODEL), None, ALU.mult)))
            for l in range(DEPTH):
                norm_u(l)
                if l == 0:
                    prepare_lower_bounds()
                for i in range(len(HG_TILES) - 1):
                    follow(l, i)
                for c in range(HEADS):
                    for s in range(steps_of(c)):
                        (hgrn if c < HG_HEADS else attend)(l, c, s)
                        if c == 0 and s == 1:
                            follow(l, len(HG_TILES) - 1)
                        if s == stack_step(c) + 1 and HG_HEADS <= c + 1 < HEADS:
                            stack_low(l * AT_HEADS + c + 1 - HG_HEADS)
                        for i in units_followed(c, s):
                            follow(l, i)
                scale_output(l * HEADS + HEADS - 1)
                for i in units_not_followed(HEADS - 1):
                    follow(l, i)
                gate_main(l, HEADS - 1)
                gate_meta(l, HEADS - 1)
                for i in range(OUT_LATE, LAYER_UNITS):
                    follow(l, i)
                    if i > OUT_C:
                        add_squares(l + 1, TILE_ORDER.index(UNITS[i][2]) - 1)
            norm_out()

        @block.tensor
        def _(pe):
            def piece(l, i, k):
                what, c, j, _ = UNITS[i]
                t = l * LAYER_UNITS + i
                if k == 0:
                    pe.wait_ge(lo_cut, t + 1)
                    if t >= 2:
                        pe.wait_ge(evacuated[t % 2], evac_count(t - 2))
                    if what == "outA":
                        pe.wait_ge(mix_lo_ready, l * HEADS + HG_HEADS)
                if i == OUT_B or (i == OUT_LATE and k == EARLY_K):
                    pe.wait_ge(mix_lo_ready, l * HEADS + HG_HEADS + k + 1)
                last_k = (EARLY_K if OUT_B <= i < OUT_LATE else KT) - 1
                if i == 0:
                    pe.wait_ge(u_lo_ready, l * KT + k + 1)
                hi, lo = (mix_hi, mix_lo) if what in ("outA", "outB") else (u_hi, u_lo)
                wh, wl = w_hi[:, t % N_CUT, k, :], w_lo[:, t % N_CUT, k, :]
                for w, x, p in ((wh, hi, 0), (wh, lo, 1), (wl, hi, 2)):
                    for n, cols_n in enumerate(halves):
                        ins = pe.matmul(proj[t % 2][:, n, both], w, x[:, k, cols_n],
                                        start=(k == 0 and p == 0), stop=(k == last_k and p == 2))
                if k == last_k:
                    ins.then_inc(unit_done, 1)

            def last_piece(l, tile):
                t = l * LAYER_UNITS + OUT_C
                if tile == 0:
                    pe.wait_ge(lo_cut, t + 1)
                elif tile == 1:
                    pe.wait_ge(evacuated[t % 2], evac_count(t - 2))
                else:
                    pe.wait_ge(last_added, l * (EARLY_TILES - 1) + tile - 1)
                wh, wl = w_hi[:, t % N_CUT, tile, :], w_lo[:, t % N_CUT, tile, :]
                for w, x, p in ((wh, mix_hi, 0), (wh, mix_lo, 1), (wl, mix_hi, 2)):
                    for n, cols_n in enumerate(halves):
                        ins = pe.matmul(last_out(l, tile)[:, n, both], w, x[:, EARLY_K, cols_n],
                                        start=(p == 0), stop=(p == 2))
                ins.then_inc(last_done if tile < EARLY_TILES - 1 else unit_done, 1)

            def feed(l, c, s):
                first, _ = fed_units(c)
                in_unit = pieces_per_unit(c)
                for q in range(pieces_by(c, s - 1), pieces_by(c, s)):
                    piece(l, first + q // in_unit, q % in_unit)

            def sum_squares(n):
                if n == 0:
                    pe.wait_ge(ones_set, 4)
                pe.wait_ge(h_sq_added, (n + 1) * (KT - 2))
                for b, cols_n in enumerate(halves):
                    pe.matmul(pair[:, b, both], ones[:, :], sq[:, cols_n], start=True, stop=False)
                pe.wait_ge(h_sq, (n + 1) * KT)
                for b, cols_n in enumerate(halves):
                    ins = pe.matmul(pair[:, b, both], ones[:, :], decay[:, (KT - 1) % 4, cols_n],
                                    start=False, stop=True)
                ins.then_inc(h_sq_summed, 1)

            def turn_v(l, c):
                if l == 0 and c == 0:
                    pe.wait_ge(consts_in, 16 * 8)
                t = l * LAYER_UNITS + FIRST_UNIT[c] + (3 if c < HG_HEADS else 2)
                pe.wait_ge(evacuated[t % 2], evac_count(t))
                if l * HEADS + c > 0:
                    pe.wait_ge(o_taken, l * HEADS + c)
                for j in range(N_CHUNKS):
                    pe.transpose(main[:, j * P:(j + 1) * P], v_t[:, chunk(j)], ident[:, :])
                pe.transpose(meta[0:N_META, 0:P], v_t[:, 0:N_META], ident[:, :]).then_inc(v_turned, 1)

            def level(g, c, lv):
                pe.wait_ge(qk_ready, g * 10 + lv + 1)
                if lv >= 2:
                    pe.wait_ge(level_read, g * LEVELS + lv - 1)
                q = qkk[:, c % 2, 0, :] if lv == 0 else qk_dec[:, lv % 2, 0, :]
                k = qk_dec[:, lv % 2, 1, :]
                if lv < META_LEVELS:
                    pe.matmul(meta[0:N_META, lv * N_META:(lv + 1) * N_META], k[:, 0:N_META],
                              q[:, 0:N_META], start=True, stop=True)
                for j in range(N_CHUNKS):
                    ins = pe.matmul(pair[:, lv % 2, j * P:(j + 1) * P], k[:, chunk(j)], q[:, chunk(j)],
                                    start=True, stop=True)
                ins.then_inc(level_done, 1)

            def turn_main(n):
                pe.wait_ge(o_scaled, n + 1)
                for j in range(N_CHUNKS):
                    ins = pe.transpose(main[:, j * P:(j + 1) * P], o_rows[:, j, :], ident[:, :])
                ins.then_inc(o_turned, 1)

            def turn_meta(n):
                pe.transpose(meta[:, 0:N_META], o_rows[0:N_META, N_CHUNKS, :], ident[0:N_META, 0:N_META])\
                    .then_inc(o_turned, 1)

            def hgrn(l, c, s):
                n, g = l * HEADS + c, l * HG_HEADS + c
                if 1 <= s <= LEVELS:
                    if s == 1 and n > 0:
                        pe.wait_ge(o_taken, n)
                        if c > 0:
                            pe.wait_ge(states_ready, g)
                    level(g, c, s - 1)
                    if s == LEVELS:
                        pe.wait_ge(meta_read, g + 1)
                        turn_v(l, c)
                elif s == TURN_KEYS:
                    pe.wait_ge(qk_ready, g * 10 + 9)
                    pe.wait_ge(level_read, g * LEVELS + 7)
                    for j in range(N_CHUNKS):
                        ins = pe.transpose(pair[:, 0, j * P:(j + 1) * P], qk_dec[:, 0, 1, chunk(j)],
                                           ident[:, :])
                    ins.then_inc(k_turned, 1)
                    pe.wait_ge(v_ready, n + 1)
                    if c > 0:
                        turn_main(n - 1)
                elif s == TURN_KEYS + 1:
                    pe.wait_ge(qk_ready, g * 10 + 10)
                    pe.wait_ge(level_read, g * LEVELS + 8)
                    for j in range(N_CHUNKS - 1):
                        pe.transpose(pair[:, 1, j * P:(j + 1) * P], qk_dec[:, 1, 1, chunk(j)], ident[:, :])
                    pe.transpose(meta[0:N_META, 0:P], qk_dec[:, 1, 1, 0:N_META], ident[:, :])\
                        .then_inc(k_turned, 1)
                    pe.wait_ge(k_ready, 2 * g + 1)
                    for j in range(N_CHUNKS):
                        ins = pe.matmul(pair[:, 0, j * P:(j + 1) * P], cols[:, j, :], v_main[:, j, :],
                                        start=True, stop=True)
                    ins.then_inc(kv_done, 1)
                elif s == TURN_KEYS + 2:
                    pe.wait_ge(k_ready, 2 * g + 2)
                    pe.matmul(pair[:, 1, 0:P], cols[0:N_META, 7, :], v_meta[:, :], start=True, stop=True)
                    for j in range(N_CHUNKS - 1):
                        ins = pe.matmul(pair[:, 1, (j + 1) * P:(j + 2) * P], cols[:, 4 + j, :],
                                        v_main[:, j, :], start=True, stop=True)
                    ins.then_inc(kv_done, 1)
                    if c > 0:
                        turn_meta(n - 1)
                elif s == HG_STEPS - 1:
                    pe.wait_ge(states_ready, g + 1)
                    if c > 0:
                        pe.wait_ge(mixed, n)
                    for j in range(N_CHUNKS):
                        out = main[:, j * P:(j + 1) * P]
                        pe.matmul(out, score[:, j, :], v_main[:, j, :], start=True, stop=False)
                        pe.matmul(out, qk_dec[:, 0, 0, chunk(j)], state_f[:, j, :], start=False,
                                  stop=(j == 3))
                        if j < 3:
                            pe.matmul(out, qk_dec[:, 1, 0, chunk(j)], state_b[:, j + 1, :],
                                      start=False, stop=True)
                    out = meta[0:N_META, 0:P]
                    pe.matmul(out, score_meta[:, :], v_meta[:, :], start=True, stop=False)
                    pe.matmul(out, qk_dec[:, 1, 0, 0:N_META], state_b[:, 0, :], start=False, stop=True)\
                        .then_inc(o_done, 1)

            def attend(l, c, s):
                n, a = l * HEADS + c, l * AT_HEADS + c - HG_HEADS
                i, comp = s // 2, s % 2
                if s == 0:
                    pe.wait_ge(stacked, 16 * 4 * (a + 1))
                    pe.wait_ge(stack_lo, 4 * (a + 1))
                    if c == HG_HEADS:
                        pe.wait_ge(states_ready, (l + 1) * HG_HEADS)
                if i < 5:
                    rows = P if i < 4 else N_META
                    cs = chunk(i) if i < 4 else slice(0, N_META)
                    part = comps[comp]
                    if s > 0:
                        pe.wait_ge(exp_done, a * 10 + s)
                    for b, keys in enumerate(halves):
                        pe.matmul(pair[0:rows, b, both], q_stack[:, comp, cs], k_stack[:, comp, keys],
                                  start=True, stop=False)
                        ins = pe.matmul(pair[0:rows, b, both], q_stack[part, comp, cs], k_low[part, keys],
                                        start=False, stop=True)
                    ins.then_inc(s_done, 1)
                if s == 1:
                    turn_v(l, c)
                if s == 2:
                    pe.wait_ge(v_ready, n + 1)
                    turn_main(n - 1)
                    turn_meta(n - 1)
                if comp == 0 and 2 <= i < 7:
                    j = i - 2
                    rows = P if j < 4 else N_META
                    pe.wait_ge(pt_ready, a * 5 + j + 1)
                    for kk in range(4):
                        pe.matmul(meta[0:rows, 0:P], cols[:, kk, 0:rows], v_main[:, kk, :],
                                  start=(kk == 0), stop=False)
                    pe.matmul(meta[0:rows, 0:P], cols[0:N_META, 4, 0:rows], v_meta[:, :],
                              start=False, stop=True).then_inc(pv_done, 1)
                if comp == 1 and 1 <= i < 6:
                    j = i - 1
                    rows = P if j < 4 else N_META
                    if j == 0:
                        pe.wait_ge(mixed, n)
                    else:
                        pe.wait_ge(pv_read, a * 4 + j)
                    pe.wait_ge(p_ready, a * 5 + j + 1)
                    p = qk_dec[0:rows, j % 2, 0, :]
                    for kk in range(4):
                        pe.transpose(main[:, kk * P:kk * P + rows], p[:, chunk(kk)], ident[0:rows, 0:rows])
                    pe.transpose(meta[0:N_META, 0:rows], p[:, 0:N_META], ident[0:rows, 0:rows])\
                        .then_inc(p_turned, 1)

            sum_squares(0)
            for l in range(DEPTH):
                for k in range(KT + 1):
                    if k < KT:
                        piece(l, 0, k)
                    if k > 0:
                        piece(l, 1, k - 1)
                for i in range(2, len(HG_TILES)):
                    for k in range(KT):
                        piece(l, i, k)
                for c in range(HEADS):
                    for s in range(steps_of(c)):
                        (hgrn if c < HG_HEADS else attend)(l, c, s)
                        feed(l, c, s)
                for k in range(EARLY_K - 2):
                    piece(l, OUT_LATE, k)
                pe.wait_ge(o_taken, (l + 1) * HEADS)
                turn_main(l * HEADS + HEADS - 1)
                turn_meta(l * HEADS + HEADS - 1)
                for k in range(EARLY_K - 2, EARLY_K):
                    piece(l, OUT_LATE, k)
                for k in range(EARLY_K):
                    piece(l, OUT_LATE + 1, k)
                piece(l, OUT_LATE, EARLY_K)
                piece(l, OUT_LATE + 1, EARLY_K)
                last_piece(l, 0)
                last_piece(l, 1)
                for i in range(OUT_C + 1, LAYER_UNITS):
                    for k in range(KT):
                        if i == OUT_C + 1 and k == KT // 2:
                            last_piece(l, 2)
                        if i == OUT_C + 1 and k == EARLY_K:
                            last_piece(l, 3)
                        piece(l, i, k)
                sum_squares(l + 1)


def packed_weights(w_in, w_out):
    units = np.empty((DEPTH * LAYER_UNITS, P, KT, P), w_in.dtype)
    turn = np.arange(P).reshape(2, 2, 32).transpose(0, 2, 1).reshape(P)
    group = {"q": 0, "zf": 1, "zb": 2, "v": 3, "g": 4, "aq": 5, "ak": 6, "av": 7, "ag": 8}
    for l in range(DEPTH):
        for i, (what, c, j, _) in enumerate(UNITS):
            if what == "outC":
                tile = w_out[l][-P:].reshape(P, KT, P).transpose(1, 0, 2).reshape(D_MODEL, P)
            elif what in ("outA", "outB"):
                rows = slice(0, D_MODEL) if what == "outA" else slice(D_MODEL, 2 * D_MODEL)
                tile = w_out[l][rows, j * P:(j + 1) * P]
            else:
                at = group[what] * D_MODEL + (c % HG_HEADS) * P
                tile = w_in[l][:, at:at + P]
                if what in ("aq", "ak"):
                    tile = tile[:, turn]
            units[l * LAYER_UNITS + i] = tile.reshape(KT, P, P).transpose(1, 0, 2)
    return units


def constants():
    s, t = np.meshgrid(np.arange(P), np.arange(P), indexing="ij")
    level = np.zeros((P, P), np.int64)
    for lv in range(1, LEVELS):
        level[(s ^ t) >= 2 ** (lv - 1)] = lv
    masks = np.stack([(level == lv) for lv in range(1, LEVELS)], axis=1).astype(np.int32)
    inv = np.float32(ROPE_THETA) ** (-np.arange(0, AT_HEAD_DIM, 2, dtype=np.float32) / np.float32(AT_HEAD_DIM))
    ang = np.arange(T, dtype=np.float32)[None, :] * inv.astype(np.float32)[:, None]
    rope = np.empty((P, 2, T), np.float32)
    row = np.arange(P)
    pair = (row % AT_HEAD_DIM) // 2
    rope[:, 0] = np.cos(ang)[pair]
    rope[:, 1] = np.sin(ang)[pair] * np.where(row % 2 == 0, -1.0, 1.0)[:, None]
    return masks, np.eye(P, dtype=np.float32), rope


def kernel(x, meta_tokens, norm_g, w_in, hg_lb_logits, hg_norm_g, diff_lambda, diff_subln_g,
           w_out, final_norm_g):
    import concourse.bacc as bacc
    from concourse.bass_utils import run_bass_kernel_spmd

    x, meta_tokens, norm_g, w_in, w_out = (np.asarray(a) for a in (x, meta_tokens, norm_g, w_in, w_out))
    hg_lb_logits, hg_norm_g, diff_lambda, diff_subln_g, final_norm_g = (
        np.asarray(a) for a in (hg_lb_logits, hg_norm_g, diff_lambda, diff_subln_g, final_norm_g))
    tokens = np.concatenate([meta_tokens, x[0]], axis=0)
    masks, identity, rope = constants()
    arrays = {
        "x_t": tokens.T.reshape(KT, P, T).transpose(1, 0, 2),
        "w_units": packed_weights(w_in, w_out),
        "norm_g": norm_g.reshape(DEPTH, KT, P).transpose(2, 0, 1),
        "lb_logits": hg_lb_logits.reshape(DEPTH, 2 * HG_HEADS, P).transpose(2, 0, 1),
        "hg_gain": hg_norm_g.T,
        "lambdas": np.broadcast_to(diff_lambda.reshape(1, DEPTH * 2, 2, AT_HEAD_DIM),
                                   (P, DEPTH * 2, 2, AT_HEAD_DIM)),
        "at_gain": diff_subln_g.T,
        "final_g": final_norm_g.reshape(KT, P).T,
        "level_masks": masks,
        "identity": identity,
        "rope": rope,
    }
    arrays = {k: np.ascontiguousarray(v) for k, v in arrays.items()}
    nc = bacc.Bacc("TRN2", target_bir_lowering=False, num_devices=1)
    args = [nc.dram_tensor(k, v.shape, mybir.dt.from_np(v.dtype), kind="ExternalInput").ap()
            for k, v in arrays.items()]
    out = nc.dram_tensor("out_t", (KT, P, SEQ), mybir.dt.float32, kind="ExternalOutput").ap()
    encoder_trunk(nc, *args, out)
    r = run_bass_kernel_spmd(nc, [arrays], core_ids=[0])
    return r.results[0]["out_t"].reshape(D_MODEL, SEQ).T.reshape(1, SEQ, D_MODEL)
```
